# Optimizing a Trainium2 kernel written in Bass

```python
import jax, jax.numpy as jnp
from jax import lax
import numpy as np

D_MODEL = 1024
BATCH = 1
SEQ = 512
DEPTH = 1

HEAD_DIM = 64
MIX_TOTAL_HEADS = D_MODEL // HEAD_DIM
N_ATTN_HEADS = MIX_TOTAL_HEADS // 2
N_MIX_GROUPS = MIX_TOTAL_HEADS - N_ATTN_HEADS
GQA_GROUP = 4
N_KV_HEADS = N_ATTN_HEADS // GQA_GROUP
ATTN_WIDTH = N_ATTN_HEADS * HEAD_DIM
MIX_WIDTH = N_MIX_GROUPS * HEAD_DIM
KV_WIDTH = N_KV_HEADS * HEAD_DIM
N_GATES = 3
IN_COLS = ATTN_WIDTH + 6 * KV_WIDTH + N_GATES * N_ATTN_HEADS + 2 * MIX_WIDTH
CMP_BLOCK = 32
CMP_STRIDE = 16
CMP_HIDDEN = 256
SEL_BLOCK = 64
SEL_TOPN = 16
SEL_Q_BLOCK = 64
WINDOW = 512
Q_BLOCK = 128
CHUNK = 128
D_FF = 4 * D_MODEL
ROPE_THETA = 10000.0
EPS = 1e-6
FORCE_SCORE = 1e9

kernel_name = "hymba_nsa_gmlp_hybrid_block"

def rms_norm(x, g):
    xf = x.astype(jnp.float32)
    y = xf * lax.rsqrt(jnp.mean(xf * xf, axis=-1, keepdims=True) + EPS)
    return (y * g.astype(jnp.float32)).astype(x.dtype)

def rope(x, pos):
    half = x.shape[-1] // 2
    inv = ROPE_THETA ** (-jnp.arange(half, dtype=jnp.float32) / half)
    ang = pos.astype(jnp.float32)[:, None] * inv[None, :]
    cos = jnp.cos(ang)[:, None, :]
    sin = jnp.sin(ang)[:, None, :]
    xf = x.astype(jnp.float32)
    x1, x2 = xf[..., :half], xf[..., half:]
    return jnp.concatenate([x1 * cos - x2 * sin, x2 * cos + x1 * sin], axis=-1).astype(x.dtype)

def masked_softmax(s, mask):
    s = jnp.where(mask, s.astype(jnp.float32), -jnp.inf)
    m = jnp.max(s, axis=-1, keepdims=True)
    m = jnp.where(jnp.isfinite(m), m, 0.0)
    p = jnp.exp(s - m)
    return p / jnp.maximum(jnp.sum(p, axis=-1, keepdims=True), 1e-20)

def compress_blocks(t, pe, w1, w2):
    B, S, Hkv, D = t.shape
    n_cmp = (S - CMP_BLOCK) // CMP_STRIDE + 1
    idx = jnp.arange(n_cmp)[:, None] * CMP_STRIDE + jnp.arange(CMP_BLOCK)[None, :]
    blk = t[:, idx] + pe[None, None, :, None, :]
    blk = jnp.swapaxes(blk, 2, 3).reshape(B, n_cmp, Hkv, CMP_BLOCK * D)
    return jax.nn.gelu(blk @ w1) @ w2

def setup_inputs(seed: int = 0) -> dict:
    key = jax.random.key(seed)
    ks = jax.random.split(key, 16)
    L = DEPTH
    nrm = jax.random.normal
    x = nrm(ks[0], (BATCH, SEQ, D_MODEL), jnp.float32)
    g_mix_norm = 1.0 + 0.02 * nrm(ks[1], (L, D_MODEL), jnp.float32)
    w_in = nrm(ks[2], (L, D_MODEL, IN_COLS), jnp.float32) * D_MODEL ** -0.5
    g_q = 1.0 + 0.02 * nrm(ks[3], (L, HEAD_DIM), jnp.float32)
    g_k = 1.0 + 0.02 * nrm(ks[4], (L, 3, HEAD_DIM), jnp.float32)
    cmp_pe = 0.5 * nrm(ks[5], (L, 2, CMP_BLOCK, HEAD_DIM), jnp.float32)
    cmp_w1 = nrm(ks[6], (L, 2, CMP_BLOCK * HEAD_DIM, CMP_HIDDEN), jnp.float32) * (CMP_BLOCK * HEAD_DIM) ** -0.5
    cmp_w2 = nrm(ks[7], (L, 2, CMP_HIDDEN, HEAD_DIM), jnp.float32) * CMP_HIDDEN ** -0.5
    g_sgu = 1.0 + 0.02 * nrm(ks[8], (L, N_MIX_GROUPS, HEAD_DIM), jnp.float32)
    sp_w = nrm(ks[9], (L, N_MIX_GROUPS, CHUNK, CHUNK), jnp.float32) * CHUNK ** -0.5
    sp_b = 1.0 + 0.1 * nrm(ks[10], (L, N_MIX_GROUPS, CHUNK), jnp.float32)
    g_out = 1.0 + 0.02 * nrm(ks[11], (L, D_MODEL), jnp.float32)
    w_out = nrm(ks[12], (L, D_MODEL, D_MODEL), jnp.float32) * D_MODEL ** -0.5
    g_ffn_norm = 1.0 + 0.02 * nrm(ks[13], (L, D_MODEL), jnp.float32)
    w_ff1 = nrm(ks[14], (L, D_MODEL, D_FF), jnp.float32) * D_MODEL ** -0.5
    w_ff2 = nrm(ks[15], (L, D_FF, D_MODEL), jnp.float32) * D_FF ** -0.5
    return {"x": x, "g_mix_norm": g_mix_norm, "w_in": w_in, "g_q": g_q, "g_k": g_k,
            "cmp_pe": cmp_pe, "cmp_w1": cmp_w1, "cmp_w2": cmp_w2, "g_sgu": g_sgu,
            "sp_w": sp_w, "sp_b": sp_b, "g_out": g_out, "w_out": w_out,
            "g_ffn_norm": g_ffn_norm, "w_ff1": w_ff1, "w_ff2": w_ff2}

def reference(x, g_mix_norm, w_in, g_q, g_k, cmp_pe, cmp_w1, cmp_w2, g_sgu,
              sp_w, sp_b, g_out, w_out, g_ffn_norm, w_ff1, w_ff2):
    B, S, _ = x.shape
    Hkv, G, D = N_KV_HEADS, GQA_GROUP, HEAD_DIM
    f32 = jnp.float32
    pos = jnp.arange(S, dtype=jnp.int32)
    scale = HEAD_DIM ** -0.5
    sizes = [ATTN_WIDTH] + [KV_WIDTH] * 6 + [N_GATES * N_ATTN_HEADS, MIX_WIDTH]
    split_pts = [int(v) for v in np.cumsum(sizes)]

    for l in range(DEPTH):
        h = rms_norm(x, g_mix_norm[l])
        z = h @ w_in[l]
        q, kc, vc, ksl, vsl, kwn, vwn, gate_logits, zu, zv = jnp.split(z, split_pts, axis=-1)

        q = rms_norm(q.reshape(B, S, N_ATTN_HEADS, D), g_q[l])
        q_rot = rope(q, pos).reshape(B, S, Hkv, G, D)
        q = q.reshape(B, S, Hkv, G, D)
        kc = kc.reshape(B, S, Hkv, D)
        vc = vc.reshape(B, S, Hkv, D)
        ksl = rope(rms_norm(ksl.reshape(B, S, Hkv, D), g_k[l, 1]), pos)
        vsl = vsl.reshape(B, S, Hkv, D)
        kwn = rope(rms_norm(kwn.reshape(B, S, Hkv, D), g_k[l, 2]), pos)
        vwn = vwn.reshape(B, S, Hkv, D)

        kcmp = rms_norm(compress_blocks(kc, cmp_pe[l, 0], cmp_w1[l, 0], cmp_w2[l, 0]), g_k[l, 0])
        vcmp = compress_blocks(vc, cmp_pe[l, 1], cmp_w1[l, 1], cmp_w2[l, 1])
        n_cmp = kcmp.shape[1]
        cmp_start = jnp.arange(n_cmp, dtype=jnp.int32) * CMP_STRIDE
        cmp_end = cmp_start + CMP_BLOCK - 1
        s_c = jnp.einsum('bshgd,bnhd->bhgsn', q, kcmp).astype(f32) * scale
        p_c = masked_softmax(s_c, cmp_end[None, :] <= pos[:, None])
        o_cmp = jnp.einsum('bhgsn,bnhd->bshgd', p_c.astype(vcmp.dtype), vcmp)

        n_sel = S // SEL_BLOCK
        top_n = min(SEL_TOPN, n_sel)
        sel_start = jnp.arange(n_sel, dtype=jnp.int32) * SEL_BLOCK
        overlap = jnp.clip(jnp.minimum(cmp_start[:, None] + CMP_BLOCK, sel_start[None, :] + SEL_BLOCK)
                           - jnp.maximum(cmp_start[:, None], sel_start[None, :]), 0).astype(f32) / CMP_BLOCK
        imp = jnp.einsum('bhgsn,nj->bhsj', p_c, overlap)
        cur = pos // SEL_BLOCK
        jj = jnp.arange(n_sel, dtype=jnp.int32)
        forced = (jj[None, :] == 0) | (jj[None, :] == cur[:, None]) | (jj[None, :] == cur[:, None] - 1)
        eligible = sel_start[None, :] <= pos[:, None]
        imp = jnp.where(forced, FORCE_SCORE, jnp.where(eligible, imp, -jnp.inf))
        top_val, top_idx = lax.top_k(imp, top_n)
        top_valid = jnp.isfinite(top_val)

        kb = ksl.reshape(B, n_sel, SEL_BLOCK, Hkv, D).transpose(0, 3, 1, 2, 4)
        vb = vsl.reshape(B, n_sel, SEL_BLOCK, Hkv, D).transpose(0, 3, 1, 2, 4)
        nqs = S // SEL_Q_BLOCK
        q_ch = q_rot.reshape(B, nqs, SEL_Q_BLOCK, Hkv, G, D).transpose(1, 0, 3, 4, 2, 5)
        idx_ch = top_idx.reshape(B, Hkv, nqs, SEL_Q_BLOCK, top_n).transpose(2, 0, 1, 3, 4)
        val_ch = top_valid.reshape(B, Hkv, nqs, SEL_Q_BLOCK, top_n).transpose(2, 0, 1, 3, 4)
        pos_ch = pos.reshape(nqs, SEL_Q_BLOCK)
        gather = jax.vmap(jax.vmap(lambda blocks, ix: blocks[ix]))

        def sel_block(args):
            qc, ic, vmask, pc = args
            kg = gather(kb, ic)
            vg = gather(vb, ic)
            s = jnp.einsum('bhgqd,bhqnkd->bhgqnk', qc, kg).astype(f32) * scale
            kpos = ic[..., None] * SEL_BLOCK + jnp.arange(SEL_BLOCK, dtype=jnp.int32)
            m = vmask[..., None] & (kpos <= pc[:, None, None])
            p = masked_softmax(s.reshape(B, Hkv, G, SEL_Q_BLOCK, top_n * SEL_BLOCK),
                               m.reshape(B, Hkv, 1, SEL_Q_BLOCK, top_n * SEL_BLOCK))
            return jnp.einsum('bhgqm,bhqmd->bhgqd', p.astype(vg.dtype),
                              vg.reshape(B, Hkv, SEL_Q_BLOCK, top_n * SEL_BLOCK, D))

        o_sel = lax.map(sel_block, (q_ch, idx_ch, val_ch, pos_ch))
        o_sel = o_sel.transpose(1, 0, 4, 2, 3, 5).reshape(B, S, Hkv, G, D)

        nqw = S // Q_BLOCK
        span = WINDOW + Q_BLOCK
        kpad = jnp.pad(kwn, ((0, 0), (WINDOW, 0), (0, 0), (0, 0)))
        vpad = jnp.pad(vwn, ((0, 0), (WINDOW, 0), (0, 0), (0, 0)))
        widx = jnp.arange(nqw, dtype=jnp.int32)[:, None] * Q_BLOCK + jnp.arange(span, dtype=jnp.int32)[None, :]
        kwin = kpad[:, widx]
        vwin = vpad[:, widx]
        kpos_w = (widx - WINDOW)[:, None, :]
        qpos_w = pos.reshape(nqw, Q_BLOCK)[:, :, None]
        mw = (kpos_w >= 0) & (kpos_w <= qpos_w) & (qpos_w - kpos_w < WINDOW)
        qw = q_rot.reshape(B, nqw, Q_BLOCK, Hkv, G, D)
        s_w = jnp.einsum('bcqhgd,bckhd->bhgcqk', qw, kwin).astype(f32) * scale
        p_w = masked_softmax(s_w, mw)
        o_win = jnp.einsum('bhgcqk,bckhd->bcqhgd', p_w.astype(vwin.dtype), vwin).reshape(B, S, Hkv, G, D)

        gates = jax.nn.sigmoid(gate_logits.astype(f32)).reshape(B, S, Hkv, G, N_GATES).astype(x.dtype)
        o_attn = (gates[..., 0:1] * o_cmp + gates[..., 1:2] * o_sel
                  + gates[..., 2:3] * o_win).reshape(B, S, ATTN_WIDTH)

        zu = jax.nn.gelu(zu)
        zv = rms_norm(jax.nn.gelu(zv).reshape(B, S, N_MIX_GROUPS, HEAD_DIM), g_sgu[l])
        zv = zv.reshape(B, S // CHUNK, CHUNK, N_MIX_GROUPS, HEAD_DIM)
        w_s = sp_w[l] * jnp.tril(jnp.ones((CHUNK, CHUNK), sp_w.dtype))
        sv = jnp.einsum('gts,bcsgd->bctgd', w_s, zv) + sp_b[l].T[:, :, None]
        o_mix = zu * sv.reshape(B, S, MIX_WIDTH)

        o = jnp.concatenate([rms_norm(o_attn, g_out[l, :ATTN_WIDTH]),
                             rms_norm(o_mix, g_out[l, ATTN_WIDTH:])], axis=-1)
        x = x + o @ w_out[l]

        h = rms_norm(x, g_ffn_norm[l])
        x = x + jnp.square(jax.nn.relu(h @ w_ff1[l])) @ w_ff2[l]
    return x


_drawn_inputs = setup_inputs


def setup_inputs(seed=0):
    import zlib

    import numpy as np

    out = dict(_drawn_inputs(seed))
    spreads = {}
    factors = {'g_mix_norm': 3.178,
     'g_q': 8.0,
     'g_k': 8.0,
     'g_sgu': 8.0,
     'g_out': 3.666,
     'g_ffn_norm': 3.625}
    for name, (base, spread) in spreads.items():
        noise = np.random.default_rng([zlib.crc32(name.encode()), seed]).standard_normal(out[name].shape)
        drawn = base * np.exp(spread * noise) if base else spread * noise
        out[name] = __import__('jax').numpy.asarray(drawn.astype(out[name].dtype))
    for name, factor in factors.items():
        out[name] = (out[name] * factor).astype(out[name].dtype)
    return out
```

```python
from contextlib import ExitStack

import concourse.bass as bass
from concourse import mybir

F32 = mybir.dt.float32
F32R = mybir.dt.float32r
BF16 = mybir.dt.bfloat16
ALU = mybir.AluOpType
ACT = mybir.ActivationFunctionType
AX = mybir.AxisListType

P = 128
SEQ, D = 512, 1024
NT = SEQ // P
NK = D // P
HD = 64
HALF = HD // 2
NH, NKV = 8, 2
GQA = NH // NKV
AW = NH * HD
NG = 8
NB = 2
CMP_STRIDE, CMP_BLOCK, CMP_HID = 16, 32, 256
NC = (SEQ - CMP_BLOCK) // CMP_STRIDE + 1
NCP = 32
FF = 4 * D
NF = FF // P
EPS = 1e-6
MASKED = -1e30
MAX_FLOOR = -1e20
SCALE = HD ** -0.5

UW = 1024
RAW = 4
HL = 6
FR = 4
CW = 3 * NH + 2 * P
GROUPS = ["A", "B", "C", "E", "D"]
K_ORDER = [4, 5, 6, 7, 0, 1, 2, 3]
STREAM = ([("split", g, u) for g in GROUPS for u in range(4)]
          + [("direct", kv, u) for kv in range(2) for u in range(4)]
          + [("split", f"O{h}", u) for h in range(2) for u in range(4)])
SPLITS = [i for i, s in enumerate(STREAM) if s[0] == "split"]
NS = len(SPLITS)
SPLIT_NO = {STREAM[i][1:]: n for n, i in enumerate(SPLITS)}
assert len(STREAM) % RAW == 0 and NF % FR == 0 and FR == RAW and (NS - FR) % HL == 0

NORMS = [(k, t) for k in ("x", "mix", "attn", "ffn") for t in range(NT)]
NORM = {n: i for i, n in enumerate(NORMS)}

SEQUENCE = [("x", 0), ("out", "A", 0), ("x", 1), ("out", "A", 1), ("x", 2), ("out", "A", 2),
            ("x", 3), ("out", "A", 3), ("q", 0), ("out", "B", 0), ("q", 1), ("out", "B", 1),
            ("q", 2), ("out", "B", 2), ("q", 3), ("out", "B", 3),
            ("gate",), ("k", 0), ("cmp_in", 0), ("k", 1), ("cmp_in", 1), ("k", 2),
            ("out", "E", 0), ("k", 3), ("out", "E", 1), ("out", "E", 2), ("out", "E", 3),
            ("out", "D", 0), ("out", "D", 1), ("out", "D", 2), ("out", "D", 3),
            ("spatial",), ("hidden",), ("kcmp",), ("vcmp",), ("kcmpT",), ("mixT", 0), ("mixT", 1),
            ("cmp_scores",), ("mixT", 2), ("mixT", 3)]
FILLS = {"x": 2, "q": 3, "k": 2, "hidden": 4, "kcmp": 1, "vcmp": 1, "kcmpT": 1, "mixT": 1}
FILL = {}
for _s in SEQUENCE:
    for _i in range(FILLS.get(_s[0], 0)):
        FILL[(*_s, _i)] = len(FILL)
for _s in [("cmpPT",)] * 2 + [("cmpO",)] * 4:
    FILL[(*_s, sum(k[0] == _s[0] for k in FILL))] = len(FILL)
FILL_KEY = list(FILL)
OUTS = [s for s in SEQUENCE if s[0] in ("out", "gate", "cmp_in")]
OUT = {s: i for i, s in enumerate(OUTS)}
LAST_OUT = {("out", g, NT - 1): g for g in "ABED"}
LAST_OUT["cmp_in", 1] = "C"
OUT_NO = {s: n for n, s in enumerate(s for s in OUTS if s not in LAST_OUT)}

STEPS = [(t, h, b) for t in range(NT) for h in range(NH) for b in range(NB)]
NV = len(STEPS)
LEAD = 3
LAG = 2


def hybrid_block(nc, x, w512, w_c, cmp_w1, cmp_w2, cmp_pe, sp_w, sp_b, g_rows, g_heads, g_sgu,
                 g_kc, rope, w_ff1, w_ff2, y):
    ctx = ExitStack()
    with ctx:
        top = [nc.sbuf_base]

        def at(name, shape, dt, offset):
            return nc.alloc_sbuf_tensor_at(name, shape, dt, offset=offset)

        def area(size):
            o = (top[0] + 31) // 32 * 32
            top[0] = o + size
            assert top[0] <= nc.sbuf_usable_end, (top[0], nc.sbuf_usable_end)
            return o

        def sb(name, shape, dt=F32):
            n = 1
            for s in shape[1:]:
                n *= s
            return at(name, shape, dt, area(n * (2 if dt == BF16 else 4)))

        raw = sb("raw", [P, RAW, UW])
        w_hi_sb = sb("w_hi_sb", [P, HL, UW], F32R)
        w_lo_sb = sb("w_lo_sb", [P, HL, UW], F32R)
        o_ht = [area(NK * SEQ * 4), area(NK * SEQ * 4)]
        ht_hi = at("ht_hi", [P, NK, SEQ], F32R, o_ht[0])
        ht_lo = at("ht_lo", [P, NK, SEQ], F32R, o_ht[1])
        o_x = area(NT * D * 4)
        xs = at("xs", [P, NT, D], F32, o_x)
        o_o = area(NT * D * 4)
        o_sb = at("o_sb", [P, NT, D], F32, o_o)
        eps_sb = sb("eps_sb", [P, 1])

        ident = sb("ident", [P, P])
        ident16 = sb("ident16", [P, P], BF16)
        causal16 = sb("causal16", [P, P], BF16)
        cmp_mask = sb("cmp_mask", [P, NT, NCP])
        spb_sb = sb("spb_sb", [P, NG])
        gkc_sb = sb("gkc_sb", [P, 1])
        glog = sb("glog", [P, NT, 3 * NH])
        ssq = sb("ssq", [P, len(NORMS)])
        rstd = sb("rstd", [P, len(NORMS)])
        hss = sb("hss", [P, 3, NT, NG])
        hrs = sb("hrs", [P, 3, NT, NG])
        ksum = sb("ksum", [P, 2])
        nmax = sb("nmax", [P, NV])
        psum_p = sb("psum_p", [P, NT, NH, NB])
        coef = sb("coef", [P, NT, NH, NB])
        cmx = sb("cmx", [P, NT * NH])
        ccf = sb("ccf", [P, NT * NH])

        o_r = area(0)
        rest = nc.sbuf_usable_end - o_r
        top[0] = o_r
        qT = sb("qT", [P, NH, SEQ], F32R)
        kT = sb("kT", [P, NB, NKV, 2, SEQ], F32R)
        qcT = sb("qcT", [P, NH // 2, SEQ])
        v_sb = sb("v_sb", [P, NT, NB, NKV * HD])
        o_t = area(18 * 1024)
        t1 = at("t1", [P, 512], F32, o_t)
        t2 = at("t2", [P, 512], F32, o_t + 2048)
        zk = at("zk", [P, NT, 256], F32, o_t + 4096)
        sqk = at("sqk", [P, 2, 256], F32, o_t + 8192)
        stack = at("stack", [P, 2, NH, 2, HD], F32, o_t + 10240)
        p_sb = at("p_sb", [P, 3, SEQ], F32, o_t)
        pt_sb = at("pt_sb", [P, 3, SEQ], F32, o_t + 3 * 2048)
        gh_sb = sb("gh_sb", [P, 3, HD])
        gsgu_sb = sb("gsgu_sb", [P, NG * HD])
        rope_sb = sb("rope_sb", [P, NT, 2, HD])
        grow = sb("grow", [P, D])
        scr = at("scr", [P, 512], F32, o_t + 6 * 2048)
        tmp = at("tmp", [P, 2, 512], F32, o_t + 7 * 2048 )
        scr2 = at("scr2", [P, D], F32, o_t)
        assert NF * SEQ * 4 <= rest
        act_sb = at("act_sb", [P, NF, SEQ], F32, o_r)
        a_hi = at("a_hi", [P, 2, SEQ], F32R, o_o)
        a_lo = at("a_lo", [P, 2, SEQ], F32R, o_o + 2 * SEQ * 4)

        par = at("par", [P, 2, NKV, SEQ // 2], F32, o_x)
        blk = at("blk", [P, 2, 16, NKV, NC], F32, o_x + 4096)
        spw_sb = at("spw_sb", [P, NG, P], F32, o_x + 12288)
        cw2_sb = sb("cw2_sb", [P, 2, 2, HD])
        pe_sb = sb("pe_sb", [P, 2, 16])
        pc = at("pc", [P, NT, NKV, GQA, NCP], F32, o_ht[0])
        pcT = at("pcT", [P, NT * NKV, P], F32, o_ht[0] + 4096)
        vblk = at("vblk", [P, NKV, GQA * HD], F32, o_ht[1])
        hid_k = at("hid_k", [P, 2, NKV, NCP], F32, o_ht[1] + 2048)
        hid_v = at("hid_v", [P, 2, NKV, GQA, NCP], F32, o_ht[1] + 2560)
        kn = at("kn", [NKV * NCP, 2, HD], F32, o_ht[1] + 4608)
        kcT = at("kcT", [P, NKV, NCP], F32, o_ht[1] + 5120)
        ksq = at("ksq", [NKV * NCP, HD], F32, o_ht[1] + 5376)

        ps = ctx.enter_context(nc.psum_tensor("ps", [P, 8, 512], F32))

        def sem(name):
            return ctx.enter_context(nc.semaphore(name))

        raw_in = [sem(f"raw_in{i}") for i in range(RAW)]
        w_hi, w_lo = sem("w_hi"), sem("w_lo")
        w_used = sem("w_used")
        cw_used = sem("cw_used")
        x_in = [sem(f"x_in{t}") for t in range(NT)]
        x_again = [sem(f"x_again{t}") for t in range(NT)]
        grow_in = sem("grow_in")
        tables_in, spat_in = sem("tables_in"), sem("spat_in")
        y_out = sem("y_out")
        eps_made, ident_made, masks_made = sem("eps_made"), sem("ident_made"), sem("masks_made")
        spw_made, pads_made = sem("spw_made"), sem("pads_made")
        n_ssq, n_root, n_rstd, n_rows = [sem(f"n_{k}") for k in ("ssq", "root", "rstd", "rows")]
        ht_half, ht_done = sem("ht_half"), sem("ht_done")
        filled = sem("filled")
        free = [sem(f"free{b}") for b in range(4)]
        out_done, out_evac = sem("out_done"), sem("out_evac")
        h_ssq, h_sum, h_root, h_step = [sem(f"h_{k}") for k in ("ssq", "sum", "root", "step")]
        rot, st_hi, st_lo = sem("rot"), sem("st_hi"), sem("st_lo")
        blk_done = sem("blk_done")
        zv_sq, zv_sum, zv_norm = sem("zv_sq"), sem("zv_sum"), sem("zv_norm")
        sp_done, mixed = sem("sp_done"), sem("mixed")
        kc_sq, kc_root, kc_rstd = [sem(f"kc_{k}") for k in ("sq", "root", "rstd")]
        cs_done, cs_step, c_exp = sem("cs_done"), sem("cs_step"), sem("c_exp")
        c_step, c_probs = sem("c_step"), sem("c_probs")
        g_exp, g_step = sem("g_exp"), sem("g_step")
        co_done = sem("co_done")
        s_done, s_max, p_done = sem("s_done"), sem("s_max"), sem("p_done")
        pt_done = sem("pt_done")
        pt_evac = [sem("pt_evac_sel"), sem("pt_evac_win")]
        pv_done = sem("pv_done")
        o_step, o_evac = sem("o_step"), sem("o_evac")
        attn_t, ffn_t = sem("attn_t"), sem("ffn_t")
        y_done, resid = sem("y_done"), sem("resid")
        bank_free = sem("bank_free")
        squared = sem("squared")
        ah_done, al_done = sem("ah_done"), sem("al_done")
        m_done, final = sem("m_done"), sem("final")

        block = ctx.enter_context(nc.Block())

        def slot_w(n, halves, size=512):
            return halves[:, n % HL, 0:2 * size].rearrange("p (k n) -> p k n", k=2)

        def three(pe, out, l_hi, l_lo, r_hi, r_lo, start, stop):
            pe.matmul(out, l_hi, r_hi, start=start, stop=False)
            pe.matmul(out, l_hi, r_lo, start=False, stop=False)
            return pe.matmul(out, l_lo, r_hi, start=False, stop=stop)

        def fill_bank(j):
            return 4 + j % 4

        def wait_free(eng, j):
            key = FILL_KEY[j]
            if key[0] in ("x", "mixT"):
                eng.wait_ge(ht_done, HTN["x" if key[0] == "x" else "mix", key[1], key[2]] + 1)
            elif key[0] == "cmpO":
                eng.wait_ge(co_done, key[1] + 1)
            else:
                eng.wait_ge(free[j % 4], sum(FILL_KEY[i][0] not in ("x", "mixT", "cmpO")
                                             for i in range(j % 4, j + 1, 4)))

        def wait_bank(eng, j):
            if j >= 4:
                wait_free(eng, j - 4)

        def wait_fill(eng, j):
            eng.wait_ge(filled, j + 1)

        def wait_out(eng, s):
            if s in LAST_OUT:
                eng.wait_ge(w_used, SPLIT_NO[LAST_OUT[s], 3] + 1)
            else:
                eng.wait_ge(out_done, OUT_NO[s] + 1)

        def bc(ap, shape):
            return ap.broadcast_to(shape)

        @block.sync
        def _(sp):
            w5 = {}
            for i, g in enumerate(["A", "B", "E", "D", "O0", "O1"]):
                for u in range(4):
                    w5[g, u] = w512[4 * i + u]

            def load(i):
                kind, g, u = STREAM[i]
                if i >= RAW:
                    was = STREAM[i - RAW]
                    if was[0] == "split":
                        sp.wait_ge(w_lo, SPLIT_NO[was[1:]] + 1)
                    elif was[2] < 3:
                        sp.wait_ge(cw_used, 3 * was[1] + was[2] + 1)
                    else:
                        sp.wait_ge(filled, FILL["hidden", 2 * was[1] + 1] + 1)
                if kind == "direct":
                    src, n = cmp_w1[g, u], UW
                elif g == "C":
                    src, n = w_c[u], 2 * CW
                else:
                    src, n = w5[g, u], UW
                sp.dma_start(raw[:, i % RAW, 0:n], src).then_inc(raw_in[i % RAW], 16)

            sp.dma_start(xs[:, 0, :], x[0]).then_inc(x_in[0], 16)
            for i in range(RAW):
                load(i)
            for t in range(1, NT):
                sp.dma_start(xs[:, t, :], x[t]).then_inc(x_in[t], 16)
            for i in range(RAW, len(STREAM)):
                load(i)
                if STREAM[i] == ("split", "O0", 0):
                    sp.wait_ge(filled, FILL["hidden", 3] + 1)
                    sp.wait_ge(sp_done, 4)
                    for t in range(NT):
                        sp.dma_start(xs[:, t, :], x[t]).then_inc(x_again[t], 16)
            with sp.Fori(0, NF // RAW) as i:
                for j in range(RAW):
                    sp.wait_ge(w_lo, i * RAW + (NS + j - RAW + 1))
                    sp.dma_start(raw[:, j, :], w_ff1[i * RAW + j]).then_inc(raw_in[j], 16)
            with sp.Fori(0, NF // RAW) as i:
                for j in range(RAW):
                    sp.wait_ge(w_lo, i * RAW + (NS + NF + j - RAW + 1))
                    sp.dma_start(raw[:, j, :], w_ff2[i * RAW + j]).then_inc(raw_in[j], 16)
            for t in range(NT):
                sp.wait_ge(final, t + 1)
                sp.dma_start(y[t], xs[:, t, :]).then_inc(y_out, 16)
            sp.wait_ge(y_out, 16 * NT)

        @block.gpsimd
        def _(pool):
            pool.dma_start(grow[:, :], g_rows[0:1, :].broadcast_to([P, D])).then_inc(grow_in, 16)
            pool.memset(eps_sb[:, :], EPS).then_inc(eps_made, 1)
            pool.memset(ident[:, :], 0.0).then_inc(ident_made, 1)
            pool.wait_ge(ident_made, 1)
            pool.affine_select(out=ident[:, :], in_=ident[:, :], compare_op=ALU.not_equal, fill=1.0,
                               base=0, pattern=[[-1, P]], channel_multiplier=1).then_inc(ident_made, 1)
            pool.dma_start(gh_sb[:, :, :], g_heads[:, :].unsqueeze(0).broadcast_to([P, 3, HD])
                           ).then_inc(tables_in, 16)
            pool.dma_start(rope_sb[:, :, :, :], rope[:, :, :, :]).then_inc(tables_in, 16)
            pool.dma_start(gsgu_sb[:, :], g_sgu[0:1, :].broadcast_to([P, NG * HD])).then_inc(tables_in, 16)
            pool.dma_start(spb_sb[:, :], sp_b[:, :]).then_inc(tables_in, 16)
            pool.dma_start(gkc_sb[:, :], g_kc[:, :]).then_inc(tables_in, 16)
            pool.dma_start(cw2_sb[:, :, :, :], cmp_w2[:, :, :, :]).then_inc(tables_in, 16)
            pool.dma_start(pe_sb[:, :, :], cmp_pe[:, :, :]).then_inc(tables_in, 16)
            pool.memset(ident16[:, :], 0.0).then_inc(masks_made, 1)
            pool.memset(causal16[:, :], 0.0).then_inc(masks_made, 1)
            pool.memset(cmp_mask[:, :, :], 0.0).then_inc(masks_made, 1)
            pool.wait_ge(masks_made, 3)
            pool.affine_select(out=ident16[:, :], in_=ident16[:, :], compare_op=ALU.not_equal, fill=1.0,
                               base=0, pattern=[[-1, P]], channel_multiplier=1).then_inc(masks_made, 1)
            pool.affine_select(out=causal16[:, :], in_=causal16[:, :], compare_op=ALU.is_ge, fill=MASKED,
                               base=0, pattern=[[-1, P]], channel_multiplier=1).then_inc(masks_made, 1)
            pool.affine_select(out=cmp_mask[:, :, :], in_=cmp_mask[:, :, :], compare_op=ALU.is_ge,
                               fill=MASKED, base=1 - CMP_BLOCK, pattern=[[P, NT], [-CMP_STRIDE, NCP]],
                               channel_multiplier=1).then_inc(masks_made, 1)
            pool.wait_ge(filled, FILL["x", NT - 1, 1] + 1)
            pool.dma_start(spw_sb[:, :, :], sp_w[:, :, :]).then_inc(spat_in, 16)
            pool.wait_ge(spat_in, 16)
            pool.affine_select(out=spw_sb[:, :, :], in_=spw_sb[:, :, :], compare_op=ALU.is_ge, fill=0.0,
                               base=0, pattern=[[0, NG], [1, P]], channel_multiplier=-1).then_inc(spw_made, 1)
            pool.wait_ge(n_rows, NT)
            pool.dma_start(grow[:, :], g_rows[1:2, :].broadcast_to([P, D])).then_inc(grow_in, 16)
            pool.wait_ge(w_used, SPLIT_NO["D", 3] + 1)
            pool.memset(vblk[:, :, :], 0.0).then_inc(pads_made, 1)
            pool.memset(hid_k[:, :, :, :], 0.0).then_inc(pads_made, 1)
            pool.memset(hid_v[:, :, :, :, :], 0.0).then_inc(pads_made, 1)
            pool.wait_ge(n_rows, 3 * NT)
            pool.dma_start(grow[:, :], g_rows[2:3, :].broadcast_to([P, D])).then_inc(grow_in, 16)

        MASKS, PADS = 6, 3

        def norm_src(kind, t):
            if kind in ("x", "ffn"):
                return xs[:, t, :]
            return o_sb[:, t, AW:] if kind == "mix" else o_sb[:, t, 0:AW]

        def norm_dst(kind, t):
            return {"x": xs[:, t, :], "ffn": o_sb[:, t, :]}.get(kind, norm_src(kind, t))

        def norm_width(kind):
            return D if kind in ("x", "ffn") else AW

        def halves_of(kind, t, i, fill):
            k0 = {"x": 4 * i, "ffn": 4 * i, "mix": 4, "attn": 0}[kind]
            src = ps[:, fill, :].rearrange("p (k s) -> p k s", k=4)
            cut = (slice(None), slice(k0, k0 + 4), slice(t * P, t * P + P))
            return src, ht_hi[cut], ht_lo[cut]

        HT = ([("x", t, i) for t in range(NT) for i in range(2)] + [("mix", t, 0) for t in range(NT)]
              + [("attn", t, 0) for t in range(NT)] + [("ffn", t, i) for t in range(NT) for i in range(2)])
        HTN = {k: n for n, k in enumerate(HT)}

        def ht_bank(kind, t, i):
            if kind == "x":
                return fill_bank(FILL["x", t, i])
            if kind == "mix":
                return fill_bank(FILL["mixT", t, 0])
            return 4 + t if kind == "attn" else 2 * (t % 2) + i

        def kstack(m, w):
            return stack[:, m % 2, :, :, :].rearrange("p h e d -> p (h e d)").rearrange(
                "p (c w e d) -> p c w e d", c=NB * NKV, w=2, e=2)[:, :, w, :, :]

        def k_dup():
            k = t1[:, 0:256].rearrange("p (c d) -> p c d", d=HD)
            return bc(k.unsqueeze(2), [P, NB * NKV, 2, HD])

        def stack_read(m):
            return FILL[("q", m, 1) if m < NT else ("k", m - NT, 1)]

        @block.scalar
        def _(act):
            def hi(n, width=UW):
                i = SPLITS[n]
                act.wait_ge(raw_in[i % RAW], 16 * (i // RAW + 1))
                if n >= HL:
                    act.wait_ge(w_used, n - HL + 1)
                act.activation(w_hi_sb[:, n % HL, 0:width], raw[:, i % RAW, 0:width], ACT.Copy
                               ).then_inc(w_hi, 1)

            def norm_sum(kind, t, scratch):
                j = NORM[kind, t]
                if j:
                    act.wait_ge(n_ssq, j)
                act.activation(scratch, norm_src(kind, t), ACT.Square,
                               accum_out=ssq[:, j:j + 1]).then_inc(n_ssq, 1)

            def norm_root(kind, t):
                j = NORM[kind, t]
                act.wait_ge(n_ssq, j + 1)
                act.activation(rstd[:, j:j + 1], ssq[:, j:j + 1], ACT.Sqrt, bias=eps_sb[:, :],
                               scale=1.0 / norm_width(kind)).then_inc(n_root, 1)

            def ht_hi_evac(kind, t, i):
                if kind in ("x", "mix"):
                    act.wait_ge(filled, FILL["x" if kind == "x" else "mixT", t, i] + 1)
                elif kind == "attn":
                    act.wait_ge(attn_t, t + 1)
                else:
                    act.wait_ge(ffn_t, 2 * t + i + 1)
                src, h, _ = halves_of(kind, t, i, ht_bank(kind, t, i))
                act.activation(h, src, ACT.Copy).then_inc(ht_half, 1)

            act.wait_ge(eps_made, 1)
            for t in range(NT):
                act.wait_ge(x_in[t], 16)
                norm_sum("x", t, o_sb[:, NT - 1, :])
                norm_root("x", t)
                if t == 0:
                    hi(0)
                for i in range(2):
                    ht_hi_evac("x", t, i)
                if t == 0:
                    hi(1)
                    hi(2)
                    hi(3)

            def stats_root(which, t):
                c = which * NT + t + 1
                act.wait_ge(h_sum, c)
                n = NH if which == 0 else NB * NKV
                act.activation(hrs[:, which, t, 0:n], hss[:, which, t, 0:n], ACT.Sqrt,
                               bias=eps_sb[:, :], scale=1.0 / HD).then_inc(h_root, 1)

            def evac_q(t):
                o = OUT["out", "A", t]
                wait_out(act, ("out", "A", t))
                act.activation(o_sb[:, t, AW:], ps[:, o % 4, :], ACT.Square).then_inc(h_ssq, 1)
                act.activation(o_sb[:, t, 0:AW], ps[:, o % 4, :], ACT.Copy).then_inc(out_evac, 1)

            def evac_kv(t):
                o = OUT["out", "B", t]
                src = ps[:, o % 4, :].rearrange("p (b w n) -> p b w n", b=NB, w=2)
                wait_out(act, ("out", "B", t))
                if t >= 2:
                    act.wait_ge(h_sum, NT + t - 1)
                act.activation(sqk[:, t % 2, :].rearrange("p (b n) -> p b n", b=NB), src[:, :, 0, :],
                               ACT.Square).then_inc(h_ssq, 1)
                act.activation(zk[:, t, :].rearrange("p (b n) -> p b n", b=NB), src[:, :, 0, :], ACT.Copy)
                act.activation(v_sb[:, t, :, :], src[:, :, 1, :], ACT.Copy).then_inc(out_evac, 1)

            def stack_hi(m):
                act.wait_ge(rot, m + 1)
                if m >= 2:
                    wait_fill(act, stack_read(m - 2))
                if m < NT:
                    act.activation(stack[:, m % 2, :, 0, :].bitcast(F32R),
                                   t1[:, :].rearrange("p (h d) -> p h d", h=NH), ACT.Copy).then_inc(st_hi, 1)
                else:
                    act.activation(kstack(m, 0).bitcast(F32R), k_dup(), ACT.Copy).then_inc(st_hi, 1)

            def fill_evac(key, i, dst, scale=1.0):
                j = FILL[(*key, i)]
                wait_fill(act, j)
                act.activation(dst, ps[:, fill_bank(j), :].rearrange("p (h s) -> p h s", h=dst.shape[1]),
                               ACT.Copy, scale=scale).then_inc(free[j % 4], 1)

            def q_evac(t):
                s = slice(t * P, t * P + P)
                fill_evac(("q", t), 0, qT[:, 0:4, s], SCALE)
                fill_evac(("q", t), 2, qcT[:, :, s])

            def k_evac(t):
                fill_evac(("k", t), 0, kT[:, 0, :, :, t * P:t * P + P].rearrange("p g w s -> p (g w) s"))

            evac_q(0)
            stats_root(0, 0)
            hi(4)
            stack_hi(0)
            evac_q(1)
            stats_root(0, 1)
            hi(5)
            stack_hi(1)
            evac_q(2)
            stats_root(0, 2)
            hi(6)
            hi(7)
            evac_q(3)
            q_evac(0)
            stack_hi(2)
            stats_root(0, 3)
            evac_kv(0)
            hi(8, 2 * CW)
            q_evac(1)
            stack_hi(3)
            stats_root(1, 0)
            evac_kv(1)
            hi(9, 2 * CW)
            q_evac(2)
            stack_hi(4)
            stats_root(1, 1)
            evac_kv(2)
            hi(10, 2 * CW)
            hi(11, 2 * CW)
            q_evac(3)
            stack_hi(5)
            stats_root(1, 2)
            evac_kv(3)
            o = OUT["gate",]
            wait_out(act, ("gate",))
            act.activation(glog[:, :, :], ps[:, o % 4, 0:NT * 3 * NH].rearrange("p (t c) -> p t c", t=NT),
                           ACT.Copy).then_inc(out_evac, 1)
            hi(12)
            hi(13)
            k_evac(0)
            stack_hi(6)
            stats_root(1, 3)

            def evac_cmp_in(kv):
                o = OUT["cmp_in", kv]
                wait_out(act, ("cmp_in", kv))
                for g in range(NKV):
                    for odd in range(2):
                        last = act.activation(par[HD * odd:HD * odd + HD, kv, g, :],
                                              ps[HD * g:HD * g + HD, o % 4, odd::2], ACT.Copy)
                last.then_inc(out_evac, 1)

            evac_cmp_in(0)
            k_evac(1)
            stack_hi(7)
            hi(14)
            hi(15)
            evac_cmp_in(1)
            k_evac(2)

            def evac_gelu(g, t):
                o = OUT["out", g, t]
                wait_out(act, ("out", g, t))
                dst = o_sb[:, t, 0:AW] if g == "E" else o_sb[:, t, AW:]
                act.activation(dst, ps[:, o % 4, :], ACT.Gelu_apprx_tanh).then_inc(out_evac, 1)

            evac_gelu("E", 0)
            hi(16)
            k_evac(3)
            evac_gelu("E", 1)
            hi(17)
            evac_gelu("E", 2)
            hi(18)
            hi(19)
            evac_gelu("E", 3)
            for t in range(NT):
                act.wait_ge(out_evac, OUT["out", "E", t] + 1)
                act.wait_ge(st_lo, 2 * NT)
                if t >= 2:
                    act.wait_ge(zv_sum, t - 1)
                act.activation((t1, t2)[t % 2][:, :], o_sb[:, t, 0:AW], ACT.Square).then_inc(zv_sq, 1)
            act.wait_ge(zv_sum, NT)
            act.activation(hrs[:, 2, :, :], hss[:, 2, :, :], ACT.Sqrt, bias=eps_sb[:, :], scale=1.0 / HD
                           ).then_inc(h_root, 1)
            for t in range(NT):
                evac_gelu("D", t)

            act.wait_ge(pads_made, PADS)
            for kv in range(2):
                for half in range(2):
                    j = FILL["hidden", 2 * kv + half]
                    act.wait_ge(filled, j + 1)
                    src = ps[:, fill_bank(j), 0:NKV * NC].rearrange("p (g n) -> p g n", g=NKV)
                    if kv == 0:
                        act.activation(hid_k[:, half, :, 0:NC], src, ACT.Gelu_apprx_tanh).then_inc(free[j % 4], 1)
                    else:
                        act.activation(hid_v[:, half, :, :, 0:NC], bc(src.unsqueeze(2), [P, NKV, GQA, NC]),
                                       ACT.Gelu_apprx_tanh).then_inc(free[j % 4], 1)

            for t in range(NT):
                act.wait_ge(mixed, 4)
                norm_sum("mix", t, t1[:, :] if t % 2 else t2[:, :])
            for t in range(NT):
                norm_root("mix", t)
            j = FILL["kcmp", 0]
            act.wait_ge(filled, j + 1)
            act.activation(ksq[:, :], ps[0:NKV * NCP, fill_bank(j), 0:HD], ACT.Square,
                           accum_out=ksum[0:NKV * NCP, 0:1]).then_inc(kc_sq, 1)
            act.wait_ge(kc_sq, 1)
            act.activation(ksum[0:NKV * NCP, 1:2], ksum[0:NKV * NCP, 0:1], ACT.Sqrt,
                           bias=eps_sb[0:NKV * NCP, :], scale=1.0 / HD).then_inc(kc_root, 1)
            j = FILL["kcmpT", 0]
            act.wait_ge(filled, j + 1)
            act.wait_ge(tables_in, 16 * 7)
            act.activation(kcT[:, :, :], ps[:, fill_bank(j), 0:NKV * NCP].rearrange("p (g n) -> p g n", g=NKV),
                           ACT.Copy, scale=gkc_sb[:, :]).then_inc(free[j % 4], 1)
            for t in range(NT):
                ht_hi_evac("mix", t, 0)
            for n in range(20, 24):
                hi(n)

            act.wait_ge(out_evac, OUT["gate",] + 1)
            act.activation(glog[:, :, :], glog[:, :, :], ACT.Exp, scale=-1.0).then_inc(g_exp, 1)
            act.wait_ge(cs_step, 5)
            act.activation(pc[:, :, :, :, :], pc[:, :, :, :, :], ACT.Exp, scale=SCALE).then_inc(c_exp, 1)

            def exp(v):
                t, h, b = STEPS[v]
                n = P * (t + 1)
                act.wait_ge(s_max, v + 1)
                if v >= 3:
                    act.wait_ge(pt_done, v - 2)
                act.activation(p_sb[:, v % 3, 0:n], ps[:, v % 4, 0:n], ACT.Exp, bias=nmax[:, v:v + 1],
                               accum_out=psum_p[:, t, h, b:b + 1]).then_inc(p_done, 1)

            def pt(v):
                n = P * (STEPS[v][0] + 1)
                act.wait_ge(pt_done, v + 1)
                if v >= 3:
                    act.wait_ge(pv_done, v - 2)
                act.activation(pt_sb[:, v % 3, 0:n], ps[:, 4 + v % 2, 0:n], ACT.Copy).then_inc(pt_evac[1], 1)

            def c_evac(i):
                j = FILL["cmpO", i]
                act.wait_ge(filled, j + 1)
                act.activation(o_sb[:, i, 0:AW], ps[:, fill_bank(j), :], ACT.Copy).then_inc(co_done, 1)

            exp(0)
            for i in range(2):
                j = FILL["cmpPT", i]
                act.wait_ge(filled, j + 1)
                act.activation(pcT[:, 4 * i:4 * i + 4, :], ps[:, fill_bank(j), :].rearrange("p (i s) -> p i s", i=4),
                               ACT.Copy).then_inc(free[j % 4], 1)
            exp(1)
            exp(2)
            for i in range(NT):
                c_evac(i)
            for v in range(LEAD, NV + LEAD):
                if v < NV:
                    exp(v)
                if (v - LEAD) % 2 == 1:
                    pt(v - LEAD)
                t = STEPS[min(v, NV - 1)][0]
                if v % 16 == 12 and t > 0:
                    act.wait_ge(o_evac, t)
                    norm_sum("attn", t - 1, scr[:, :])
                if v == 40:
                    hi(24)
                if v == 44:
                    hi(25)
            for t in range(NT - 1):
                norm_root("attn", t)
            act.wait_ge(o_evac, NT)
            norm_sum("attn", NT - 1, scr[:, :])
            norm_root("attn", NT - 1)
            for t in range(NT):
                ht_hi_evac("attn", t, 0)
            hi(26)
            hi(27)

            def f_hi(slot, count, used):
                act.wait_ge(raw_in[slot], count)
                act.wait_ge(w_used, used)
                act.activation(w_hi_sb[:, slot, :], raw[:, slot, :], ACT.Copy).then_inc(w_hi, 1)

            IN0 = 16 * (len(STREAM) // RAW)
            for t in range(NT):
                act.wait_ge(resid, NT + t + 1)
                norm_sum("ffn", t, scr2[:, :])
                norm_root("ffn", t)
                for i in range(2):
                    ht_hi_evac("ffn", t, i)
                if t == NT - 2:
                    for j in range(FR - 1):
                        f_hi(j, IN0 + 16, NS - FR + j + 1)
            f_hi(FR - 1, IN0 + 16, NS)

            def relu(f):
                i, j = f
                act.wait_ge(w_used, i * FR + (NS + j + 1))
                act.activation(act_sb[:, i * FR + j, :], ps[:, 4 + j, :], ACT.Relu).then_inc(bank_free, 1)

            with act.Fori(0, NF // FR - 1) as i:
                for j in range(FR):
                    relu((i, j))
                    f_hi(j, i * 16 + (IN0 + 32), i * FR + (NS + j + 1))

            IN1 = IN0 + 16 * (NF // RAW)

            def a_half(slot, f, used, squares):
                act.wait_ge(w_used, used)
                act.wait_ge(squared, squares)
                act.activation(a_hi[:, slot, :], act_sb[:, f, :], ACT.Copy).then_inc(ah_done, 1)

            for j in range(FR):
                relu((NF // FR - 1, j))
                f_hi(j, IN1 + 16, NS + NF - FR + j + 1)
                if j < 2:
                    a_half(j, j, NS + NF - FR, j + 1)
            with act.Fori(0, NF // FR - 1) as i:
                for j in range(FR):
                    a_half(j % 2, i * FR + (j + 2), i * FR + (NS + NF + j + 1), i * FR + (j + 3))
                    f_hi(j, i * 16 + (IN1 + 32), i * FR + (NS + NF + j + 1))
            for f in (NF - 2, NF - 1):
                a_half(f % 2, f, NS + NF + f - 1, f + 1)

        @block.vector
        def _(dve):
            def lo(n, width=UW):
                i = SPLITS[n]
                dve.wait_ge(w_hi, n + 1)
                dve.tensor_tensor(w_lo_sb[:, n % HL, 0:width], raw[:, i % RAW, 0:width],
                                  w_hi_sb[:, n % HL, 0:width].bitcast(F32), ALU.subtract).then_inc(w_lo, 1)

            def norm_inv(kind, t):
                j = NORM[kind, t]
                dve.wait_ge(n_root, j + 1)
                dve.reciprocal(rstd[:, j:j + 1], rstd[:, j:j + 1]).then_inc(n_rstd, 1)

            def norm_rows(kind, t):
                j = NORM[kind, t]
                cols = {"mix": slice(AW, D), "attn": slice(0, AW)}.get(kind, slice(0, D))
                dve.wait_ge(grow_in, {"x": 16, "ffn": 48}.get(kind, 32))
                dve.wait_ge(n_rstd, j + 1)
                dve.scalar_tensor_tensor(out=norm_dst(kind, t), in0=norm_src(kind, t), scalar=rstd[:, j:j + 1],
                                         in1=grow[:, cols], op0=ALU.mult, op1=ALU.mult).then_inc(n_rows, 1)

            def ht_lo_evac(kind, t, i):
                n = HTN[kind, t, i]
                dve.wait_ge(ht_half, n + 1)
                src, h, l = halves_of(kind, t, i, ht_bank(kind, t, i))
                dve.tensor_tensor(l, src, h.bitcast(F32), ALU.subtract).then_inc(ht_done, 1)

            for t in range(NT):
                norm_inv("x", t)
                norm_rows("x", t)
                if t == 0:
                    lo(0)
                ht_lo_evac("x", t, 0)
                ht_lo_evac("x", t, 1)
                if t == 0:
                    lo(1)
                    lo(2)
                    lo(3)
            dve.wait_ge(tables_in, 16 * 7)
            steps = [0]

            def link(ins):
                steps[0] += 1
                ins.then_inc(h_step, 1)
                dve.wait_ge(h_step, steps[0])

            def heads(m):
                t = m % NT
                if m < NT:
                    return (o_sb[:, t, 0:AW].rearrange("p (h d) -> p h d", h=NH),
                            o_sb[:, t, AW:].rearrange("p (h d) -> p h d", h=NH), NH)
                return (zk[:, t, :].rearrange("p (c d) -> p c d", d=HD),
                        sqk[:, t % 2, :].rearrange("p (c d) -> p c d", d=HD), NB * NKV)

            def head_sum(m):
                _, sq, n = heads(m)
                dve.wait_ge(h_ssq, m + 1)
                dve.tensor_reduce(hss[:, m // NT, m % NT, 0:n], sq, AX.X, ALU.add).then_inc(h_sum, 1)

            def rotate(m):
                z, _, n = heads(m)
                w, t = m // NT, m % NT
                dve.wait_ge(h_root, m + 1)
                r = hrs[:, w, t, 0:n]
                link(dve.reciprocal(r, r))
                wait_evac(m)
                link(dve.tensor_tensor(z, z, bc(r.unsqueeze(2), [P, n, HD]), ALU.mult))
                if w == 0:
                    link(dve.tensor_tensor(z, z, bc(gh_sb[:, 0:1, :], [P, n, HD]), ALU.mult))
                else:
                    z4 = z.rearrange("p (b g) d -> p b g d", b=NB)
                    link(dve.tensor_tensor(z4, z4, bc(gh_sb[:, 1:3, :].unsqueeze(2), [P, NB, NKV, HD]), ALU.mult))
                if m:
                    dve.wait_ge(st_lo, m)
                a = t1[:, 0:n * HD].rearrange("p (h d) -> p h d", d=HD)
                b = t2[:, 0:n * HD].rearrange("p (h d) -> p h d", d=HD)
                dve.tensor_tensor(a, z, bc(rope_sb[:, t, 0:1, :], [P, n, HD]), ALU.mult)
                dve.tensor_tensor(b[:, :, 0:HALF], z[:, :, HALF:], bc(rope_sb[:, t, 1:2, 0:HALF], [P, n, HALF]), ALU.mult)
                link(dve.tensor_tensor(b[:, :, HALF:], z[:, :, 0:HALF], bc(rope_sb[:, t, 1:2, HALF:], [P, n, HALF]), ALU.mult))
                dve.tensor_tensor(a, a, b, ALU.add).then_inc(rot, 1)

            def wait_evac(m):
                s = ("out", "A", m) if m < NT else ("out", "B", m - NT)
                dve.wait_ge(out_evac, OUT[s] + 1)

            def stack_lo(m):
                dve.wait_ge(st_hi, m + 1)
                if m < NT:
                    s = stack[:, m % 2]
                    dve.tensor_tensor(s[:, :, 1, :].bitcast(F32R), t1[:, :].rearrange("p (h d) -> p h d", h=NH),
                                      s[:, :, 0, :], ALU.subtract).then_inc(st_lo, 1)
                else:
                    dve.tensor_tensor(kstack(m, 1).bitcast(F32R), k_dup(), kstack(m, 0), ALU.subtract
                                      ).then_inc(st_lo, 1)

            def q_evac(t):
                j = FILL["q", t, 1]
                wait_fill(dve, j)
                dve.tensor_scalar(qT[:, 4:8, t * P:t * P + P], ps[:, fill_bank(j), :].rearrange("p (h s) -> p h s", h=4),
                                  SCALE, None, ALU.mult).then_inc(free[j % 4], 1)

            def k_evac(t):
                j = FILL["k", t, 1]
                wait_fill(dve, j)
                dve.tensor_copy(kT[:, 1, :, :, t * P:t * P + P].rearrange("p g w s -> p (g w) s"),
                                ps[:, fill_bank(j), :].rearrange("p (h s) -> p h s", h=4)).then_inc(free[j % 4], 1)

            head_sum(0)
            lo(4)
            rotate(0)
            stack_lo(0)
            head_sum(1)
            lo(5)
            rotate(1)
            stack_lo(1)
            head_sum(2)
            lo(6)
            rotate(2)
            lo(7)
            q_evac(0)
            stack_lo(2)
            head_sum(3)
            rotate(3)
            lo(8, 2 * CW)
            q_evac(1)
            stack_lo(3)
            head_sum(4)
            rotate(4)
            lo(9, 2 * CW)
            q_evac(2)
            stack_lo(4)
            head_sum(5)
            rotate(5)
            lo(10, 2 * CW)
            lo(11, 2 * CW)
            q_evac(3)
            stack_lo(5)
            head_sum(6)
            rotate(6)
            lo(12)
            lo(13)
            k_evac(0)
            stack_lo(6)
            head_sum(7)
            rotate(7)
            k_evac(1)
            stack_lo(7)
            lo(14)
            lo(15)
            k_evac(2)

            def blocks(kv):
                dve.wait_ge(out_evac, OUT["cmp_in", kv] + 1)
                for half in range(2):
                    src = par[:, kv, :, :].rearrange("p g (n e) -> p e g n", e=8)[:, :, :, half:half + NC]
                    pe = pe_sb[:, kv, 8 * half:8 * half + 8]
                    last = dve.tensor_tensor(blk[:, kv, 8 * half:8 * half + 8, :, :], src,
                                             bc(pe.unsqueeze(2).unsqueeze(3), [P, 8, NKV, NC]), ALU.add)
                last.then_inc(blk_done, 1)

            blocks(0)
            lo(16)
            k_evac(3)
            blocks(1)
            lo(17)
            lo(18)
            lo(19)
            for t in range(NT):
                dve.wait_ge(zv_sq, t + 1)
                dve.tensor_reduce(hss[:, 2, t, :], (t1, t2)[t % 2][:, :].rearrange("p (h d) -> p h d", h=NG),
                                  AX.X, ALU.add).then_inc(zv_sum, 1)
            dve.wait_ge(h_root, 2 * NT + 1)
            link(dve.reciprocal(hrs[:, 2, :, :], hrs[:, 2, :, :]))
            for t in range(NT):
                z = o_sb[:, t, 0:AW].rearrange("p (h d) -> p h d", h=NG)
                link(dve.tensor_tensor(z, z, bc(hrs[:, 2, t, :].unsqueeze(2), [P, NG, HD]), ALU.mult))
                dve.tensor_tensor(o_sb[:, t, 0:AW], o_sb[:, t, 0:AW], gsgu_sb[:, :], ALU.mult).then_inc(zv_norm, 1)
            dve.wait_ge(out_evac, len(OUTS))
            for i in range(4):
                dve.wait_ge(sp_done, i + 1)
                for g in (2 * i, 2 * i + 1):
                    zu = o_sb[:, :, AW + g * HD:AW + g * HD + HD]
                    src = ps[:, i, (g % 2) * 256:(g % 2) * 256 + 256].rearrange("p (c d) -> p c d", c=NT)
                    last = dve.scalar_tensor_tensor(out=zu, in0=src, scalar=spb_sb[:, g:g + 1], in1=zu,
                                                    op0=ALU.add, op1=ALU.mult)
                last.then_inc(mixed, 1)
            R = NKV * NCP
            dve.wait_ge(kc_root, 1)
            dve.reciprocal(ksum[0:R, 1:2], ksum[0:R, 1:2]).then_inc(kc_rstd, 1)
            dve.wait_ge(kc_rstd, 1)
            j = FILL["kcmp", 0]
            dve.tensor_scalar(kn[:, :, :], bc(ps[0:R, fill_bank(j), 0:HD].unsqueeze(1), [R, 2, HD]),
                              ksum[0:R, 1:2], None, ALU.mult).then_inc(free[j % 4], 1)
            j = FILL["vcmp", 0]
            wait_fill(dve, j)
            dve.wait_ge(pads_made, PADS)
            for g in range(NKV):
                for r in range(GQA):
                    last = dve.tensor_copy(vblk[NCP * r:NCP * r + NCP, g, r * HD:r * HD + HD],
                                           ps[NCP * r:NCP * r + NCP, fill_bank(j), g * HD:g * HD + HD])
            last.then_inc(free[j % 4], 1)
            for t in range(NT):
                norm_inv("mix", t)
                norm_rows("mix", t)
            for t in range(NT):
                ht_lo_evac("mix", t, 0)
            for n in range(20, 24):
                lo(n)
            dve.wait_ge(cs_done, 1)
            dve.wait_ge(masks_made, MASKS)
            pairs = pc[:, :, :, :, :].rearrange("p t g h n -> p t (g h) n").rearrange(
                "p t (r e) n -> p t r e n", e=2)
            for e in range(2):
                src = ps[:, e, :].rearrange("p (t r n) -> p t r n", t=NT, n=NCP)
                dve.tensor_tensor(pairs[:, :, :, e, :], src,
                                  bc(cmp_mask[:, :, :].unsqueeze(2), [P, NT, NH // 2, NCP]), ALU.add
                                  ).then_inc(cs_step, 1)
            dve.wait_ge(cs_step, 2)
            rows = pc[:, :, :, :, :].rearrange("p t g h n -> p (t g h) n")
            dve.tensor_reduce(cmx[:, :], rows, AX.X, ALU.max).then_inc(cs_step, 1)
            dve.wait_ge(cs_step, 3)
            dve.tensor_scalar(cmx[:, :], cmx[:, :], MAX_FLOOR, None, ALU.max).then_inc(cs_step, 1)
            dve.wait_ge(cs_step, 4)
            dve.tensor_tensor(rows, rows, bc(cmx[:, :].unsqueeze(2), [P, NT * NH, NCP]), ALU.subtract
                              ).then_inc(cs_step, 1)
            dve.wait_ge(g_exp, 1)
            dve.tensor_scalar(glog[:, :, :], glog[:, :, :], 1.0, None, ALU.add).then_inc(g_step, 1)
            dve.wait_ge(g_step, 1)
            dve.reciprocal(glog[:, :, :], glog[:, :, :]).then_inc(g_step, 1)

            def row_max(v):
                n = P * (STEPS[v][0] + 1)
                dve.wait_ge(s_done, v + 1)
                dve.tensor_reduce(nmax[:, v:v + 1], ps[:, v % 4, 0:n], AX.X, ALU.max, negate=True
                                  ).then_inc(s_max, 1)

            for v in range(LEAD):
                row_max(v)
            dve.wait_ge(c_exp, 1)
            dve.wait_ge(g_step, 2)
            gates = glog[:, :, :].rearrange("p t (h n) -> p t h n", n=3)
            dve.tensor_reduce(ccf[:, :], rows, AX.X, ALU.add).then_inc(c_step, 1)
            dve.wait_ge(c_step, 1)
            dve.tensor_scalar(ccf[:, :], ccf[:, :], 1e-20, None, ALU.max).then_inc(c_step, 1)
            dve.wait_ge(c_step, 2)
            dve.reciprocal(ccf[:, :], ccf[:, :]).then_inc(c_step, 1)
            dve.wait_ge(c_step, 3)
            c3 = ccf[:, :].rearrange("p (t h) -> p t h", t=NT)
            dve.tensor_tensor(c3, c3, gates[:, :, :, 0], ALU.mult).then_inc(c_step, 1)
            dve.wait_ge(c_step, 4)
            dve.tensor_tensor(rows, rows, bc(ccf[:, :].unsqueeze(2), [P, NT * NH, NCP]), ALU.mult
                              ).then_inc(c_probs, 1)

            def pt(v):
                n = P * (STEPS[v][0] + 1)
                dve.wait_ge(pt_done, v + 1)
                if v >= 3:
                    dve.wait_ge(pv_done, v - 2)
                dve.tensor_copy(pt_sb[:, v % 3, 0:n], ps[:, 4 + v % 2, 0:n]).then_inc(pt_evac[0], 1)

            osteps = [0]

            def olink(ins):
                osteps[0] += 1
                ins.then_inc(o_step, 1)
                dve.wait_ge(o_step, osteps[0])

            def combine(t):
                c = coef[:, t, :, :]
                dve.wait_ge(p_done, 16 * t + 16)
                olink(dve.tensor_scalar(c, psum_p[:, t, :, :], 1e-20, None, ALU.max))
                olink(dve.reciprocal(c, c))
                olink(dve.tensor_tensor(c, c, gates[:, t, :, 1:3], ALU.mult))
                dve.wait_ge(co_done, t + 1)
                dve.wait_ge(pv_done, 16 * t + 16)
                for b in range(NB):
                    last = dve.tensor_tensor(tmp[:, b, :].rearrange("p (h d) -> p h d", h=NH),
                                             ps[:, 6 + b, :].rearrange("p (h d) -> p h d", h=NH),
                                             bc(c[:, :, b:b + 1], [P, NH, HD]), ALU.mult)
                olink(last)
                olink(dve.tensor_tensor(tmp[:, 0, :], tmp[:, 0, :], tmp[:, 1, :], ALU.add))
                dve.tensor_tensor(o_sb[:, t, 0:AW], o_sb[:, t, 0:AW], tmp[:, 0, :], ALU.add).then_inc(o_evac, 1)

            for v in range(LEAD, NV + LEAD):
                if v < NV:
                    row_max(v)
                if (v - LEAD) % 2 == 0:
                    pt(v - LEAD)
                if v == 42:
                    lo(24)
                if v == 46:
                    lo(25)
                if v % 16 == 20 % 16 and v >= 20:
                    combine((v - 20) // 16)
            combine(NT - 1)
            for t in range(NT - 1):
                norm_inv("attn", t)
                norm_rows("attn", t)
            norm_inv("attn", NT - 1)
            norm_rows("attn", NT - 1)
            for t in range(NT):
                ht_lo_evac("attn", t, 0)
            lo(26)
            lo(27)

            def add_residual(half, t):
                if (half, t) in ((0, NT - 1), (1, NT - 1)):
                    dve.wait_ge(w_used, SPLIT_NO[f"O{half}", 3] + 1)
                else:
                    dve.wait_ge(y_done, half * (NT - 1) + t + 1)
                if half == 0:
                    dve.wait_ge(x_again[t], 16)
                c = slice(half * 512, half * 512 + 512)
                ins = dve.tensor_tensor(xs[:, t, c], xs[:, t, c], ps[:, 4 * half + t, :], ALU.add)
                ins.then_inc(resid, 1)

            def f_lo(slot, count):
                dve.wait_ge(w_hi, count)
                dve.tensor_tensor(w_lo_sb[:, slot, :], raw[:, slot, :], w_hi_sb[:, slot, :].bitcast(F32),
                                  ALU.subtract).then_inc(w_lo, 1)

            for t in range(NT):
                add_residual(0, t)
            for t in range(NT):
                add_residual(1, t)
                norm_inv("ffn", t)
                norm_rows("ffn", t)
                ht_lo_evac("ffn", t, 0)
                ht_lo_evac("ffn", t, 1)
                if t == NT - 2:
                    for j in range(FR - 1):
                        f_lo(j, NS + j + 1)
            f_lo(FR - 1, NS + FR)

            def square(i, j):
                f = i * FR + j
                dve.wait_ge(bank_free, i * FR + (j + 1))
                dve.tensor_tensor(act_sb[:, f, :], act_sb[:, f, :], act_sb[:, f, :], ALU.mult).then_inc(squared, 1)

            def a_low(slot, f, count):
                dve.wait_ge(ah_done, count)
                dve.tensor_tensor(a_lo[:, slot, :], act_sb[:, f, :], a_hi[:, slot, :].bitcast(F32),
                                  ALU.subtract).then_inc(al_done, 1)

            with dve.Fori(0, NF // FR - 1) as i:
                for j in range(FR):
                    square(i, j)
                    f_lo(j, i * FR + (NS + FR + j + 1))
            for j in range(FR):
                square(NF // FR - 1, j)
                f_lo(j, NS + NF + j + 1)
                if j < 2:
                    a_low(j, j, j + 1)
            with dve.Fori(0, NF // FR - 1) as i:
                for j in range(FR):
                    a_low(j % 2, i * FR + (j + 2), i * FR + (j + 3))
                    f_lo(j, i * FR + (NS + NF + FR + j + 1))
            for f in (NF - 2, NF - 1):
                a_low(f % 2, f, f + 1)
            for t in range(NT):
                dve.wait_ge(m_done, t + 1)
                dve.tensor_tensor(xs[:, t, :].rearrange("p (b n) -> p b n", b=2),
                                  xs[:, t, :].rearrange("p (b n) -> p b n", b=2), ps[:, 2 * t:2 * t + 2, :],
                                  ALU.add).then_inc(final, 1)

        @block.tensor
        def _(pe):
            pe.wait_ge(ident_made, 2)

            def rows_t(kind, t):
                pe.wait_ge(n_rows, NORM[kind, t] + 1)
                src = norm_dst(kind, t)
                for i in range(norm_width(kind) // 512):
                    bank = ht_bank(kind, t, i)
                    if kind in ("x", "mix"):
                        wait_bank(pe, FILL["x" if kind == "x" else "mixT", t, i])
                    elif kind == "attn" and t < 2:
                        pe.wait_ge(pt_evac[t], NV // 2)
                    elif kind == "attn":
                        pe.wait_ge(o_evac, NT)
                    elif t >= 2:
                        pe.wait_ge(ht_done, HTN["ffn", t - 2, i] + 1)
                    else:
                        pe.wait_ge(resid, NT)
                    for k in range(4):
                        c = (4 * i + k) * P
                        last = pe.transpose(ps[:, bank, k * P:k * P + P], src[:, c:c + P], ident[:, :])
                    last.then_inc({"attn": attn_t, "ffn": ffn_t}.get(kind, filled), 1)

            def output(g, t):
                s = ("out", g, t)
                o = OUT[s]
                if o >= 4:
                    pe.wait_ge(out_evac, o - 3)
                if g == "A":
                    pe.wait_ge(ht_done, 2 * t + 2)
                for u in range(4):
                    n = SPLIT_NO[g, u]
                    if t == 0:
                        pe.wait_ge(w_lo, n + 1)
                    wh, wl = slot_w(n, w_hi_sb), slot_w(n, w_lo_sb)
                    for k in range(2):
                        c = (slice(None), 2 * u + k, slice(t * P, t * P + P))
                        last = three(pe, ps[:, o % 4, :], ht_hi[c], ht_lo[c], wh[:, k, :], wl[:, k, :],
                                     u + k == 0, u == 3 and k == 1)
                    if t == NT - 1:
                        last.then_inc(w_used, 1)
                if t < NT - 1:
                    last.then_inc(out_done, 1)

            def gate():
                o = OUT["gate",]
                pe.wait_ge(out_evac, o - 3)
                pe.wait_ge(w_lo, SPLIT_NO["C", 3] + 1)
                for t in range(NT):
                    for kt in range(NK):
                        n = SPLIT_NO["C", kt // 2]
                        c = (slice(None), kt, slice(t * P, t * P + P))
                        last = three(pe, ps[:, o % 4, t * 3 * NH:(t + 1) * 3 * NH], ht_hi[c], ht_lo[c],
                                     slot_w(n, w_hi_sb, CW)[:, kt % 2, 0:3 * NH],
                                     slot_w(n, w_lo_sb, CW)[:, kt % 2, 0:3 * NH], kt == 0, kt == NK - 1)
                last.then_inc(out_done, 1)

            def cmp_in(kv):
                o = OUT["cmp_in", kv]
                pe.wait_ge(out_evac, o - 3)
                for kt in range(NK):
                    n = SPLIT_NO["C", kt // 2]
                    c = slice(3 * NH + kv * P, 3 * NH + kv * P + P)
                    last = three(pe, ps[:, o % 4, :], slot_w(n, w_hi_sb, CW)[:, kt % 2, c],
                                 slot_w(n, w_lo_sb, CW)[:, kt % 2, c], ht_hi[:, kt, :], ht_lo[:, kt, :],
                                 kt == 0, kt == NK - 1)
                    if kv == 1 and kt % 2 == 1:
                        last.then_inc(w_used, 1)
                if kv == 0:
                    last.then_inc(out_done, 1)

            def stack_t(m):
                kind, t = ("q", m) if m < NT else ("k", m - NT)
                pe.wait_ge(st_lo, m + 1)
                s = stack[:, m % 2].rearrange("p h e d -> p (h e d)")
                for i in range(FILLS[kind]):
                    j = FILL[kind, t, i]
                    wait_bank(pe, j)
                    for k in range(4):
                        src = s[:, (4 * i + k) * P:(4 * i + k + 1) * P] if i < 2 else o_sb[:, t, k * P:k * P + P]
                        last = pe.transpose(ps[:, fill_bank(j), k * P:k * P + P], src, ident[:, :])
                    last.then_inc(filled, 1)

            def spatial():
                pe.wait_ge(out_evac, len(OUTS))
                pe.wait_ge(spw_made, 1)
                pe.wait_ge(zv_norm, NT)
                for g in range(NG):
                    mm = pe.matmul(ps[:, g // 2, (g % 2) * 256:(g % 2) * 256 + 256], spw_sb[:, g, :],
                                   o_sb[:, :, g * HD:g * HD + HD], start=True, stop=True)
                    if g % 2:
                        mm.then_inc(sp_done, 1)

            def hidden():
                for kv in range(2):
                    pe.wait_ge(blk_done, kv + 1)
                    for half in range(2):
                        wait_bank(pe, FILL["hidden", 2 * kv + half])
                    for u in range(4):
                        i = STREAM.index(("direct", kv, u))
                        pe.wait_ge(raw_in[i % RAW], 16 * (i // RAW + 1))
                        for half in range(2):
                            bank = fill_bank(FILL["hidden", 2 * kv + half])
                            for j in range(4):
                                c = j * CMP_HID + half * P
                                last = pe.matmul(ps[:, bank, 0:NKV * NC], raw[:, i % RAW, c:c + P],
                                                 blk[:, kv, 4 * u + j, :, :].rearrange("p g n -> p (g n)"),
                                                 start=u + j == 0, stop=u == 3 and j == 3)
                            if u == 3:
                                last.then_inc(filled, 1)
                        if u < 3:
                            last.then_inc(cw_used, 1)

            def kcmp():
                j = FILL["kcmp", 0]
                wait_bank(pe, j)
                for half in range(2):
                    wait_free(pe, FILL["hidden", half])
                    mm = pe.matmul(ps[0:NKV * NCP, fill_bank(j), 0:HD], hid_k[:, half, :, :].rearrange("p g n -> p (g n)"),
                                   cw2_sb[:, 0, half, :], start=half == 0, stop=half == 1)
                mm.then_inc(filled, 1)

            def vcmp():
                j = FILL["vcmp", 0]
                wait_bank(pe, j)
                for half in range(2):
                    wait_free(pe, FILL["hidden", 2 + half])
                for g in range(NKV):
                    for half in range(2):
                        mm = pe.matmul(ps[:, fill_bank(j), g * HD:g * HD + HD],
                                       hid_v[:, half, g, :, :].rearrange("p r n -> p (r n)"),
                                       cw2_sb[:, 1, half, :], start=half == 0, stop=half == 1)
                mm.then_inc(filled, 1)

            def kcmp_t():
                j = FILL["kcmpT", 0]
                wait_bank(pe, j)
                wait_free(pe, FILL["kcmp", 0])
                R = NKV * NCP
                pe.transpose(ps[:, fill_bank(j), 0:R], kn[:, :, :].rearrange("p e d -> p (e d)"), ident[0:R, 0:R]
                             ).then_inc(filled, 1)

            def cmp_scores():
                wait_free(pe, FILL["kcmpT", 0])
                pe.wait_ge(mixed, 4)
                for t in range(NT):
                    for h in range(NH):
                        e = slice(HD * (h % 2), HD * (h % 2) + HD)
                        c = (t * (NH // 2) + h // 2) * NCP
                        mm = pe.matmul(ps[:, h % 2, c:c + NCP], qcT[e, h // 2, t * P:t * P + P],
                                       kcT[e, h // GQA, :], start=True, stop=True)
                mm.then_inc(cs_done, 1)

            RUN = {"x": lambda t: rows_t("x", t), "out": output, "q": stack_t, "k": lambda t: stack_t(NT + t),
                   "gate": gate, "cmp_in": cmp_in, "spatial": spatial, "hidden": hidden, "kcmp": kcmp,
                   "vcmp": vcmp, "kcmpT": kcmp_t, "mixT": lambda t: rows_t("mix", t), "cmp_scores": cmp_scores}
            for s in SEQUENCE:
                RUN[s[0]](*s[1:])

            def scores(v):
                t, h, b = STEPS[v]
                n = P * (t + 1)
                if v < 2:
                    pe.wait_ge(cs_step, 2)
                elif v >= 4:
                    pe.wait_ge(p_done, v - 3)
                bank, q = v % 4, qT[:, h, t * P:t * P + P]
                pe.matmul(ps[:, bank, 0:n], q, kT[:, b, h // GQA, 0, 0:n], start=True, stop=False)
                pe.matmul(ps[:, bank, 0:n], q, kT[:, b, h // GQA, 1, 0:n], start=False, stop=False)
                pe.matmul(ps[:, bank, n - P:n], ident16[:, :], causal16[:, :], start=False, stop=True
                          ).then_inc(s_done, 1)

            def probs_t(v):
                pe.wait_ge(p_done, v + 1)
                if v >= 2:
                    pe.wait_ge(pt_evac[v % 2], v // 2)
                for k in range(STEPS[v][0] + 1):
                    mm = pe.transpose(ps[:, 4 + v % 2, k * P:k * P + P], p_sb[:, v % 3, k * P:k * P + P], ident[:, :])
                mm.then_inc(pt_done, 1)

            def values(v):
                t, h, b = STEPS[v]
                pe.wait_ge(pt_evac[v % 2], v // 2 + 1)
                if h == 0 and t > 0:
                    pe.wait_ge(o_evac, t)
                g = h // GQA
                for k in range(t + 1):
                    mm = pe.matmul(ps[:, 6 + b, h * HD:h * HD + HD], pt_sb[:, v % 3, k * P:k * P + P],
                                   v_sb[:, k, b, g * HD:g * HD + HD], start=k == 0, stop=k == t)
                mm.then_inc(pv_done, 1)

            pe.wait_ge(masks_made, MASKS)
            for v in range(LEAD):
                scores(v)
            pe.wait_ge(c_probs, 1)
            for i in range(2):
                j = FILL["cmpPT", i]
                wait_bank(pe, j)
                for k in range(4):
                    t, g = 2 * i + k // 2, k % 2
                    mm = pe.transpose(ps[:, fill_bank(j), k * P:k * P + P],
                                      pc[:, t, g, :, :].rearrange("p h n -> p (h n)"), ident[:, :])
                mm.then_inc(filled, 1)
            for t in range(NT):
                j = FILL["cmpO", t]
                wait_bank(pe, j)
                wait_free(pe, FILL["cmpPT", t // 2])
                for g in range(NKV):
                    mm = pe.matmul(ps[:, fill_bank(j), g * 256:g * 256 + 256], pcT[:, 2 * t + g, :],
                                   vblk[:, g, :], start=True, stop=True)
                mm.then_inc(filled, 1)
            pe.wait_ge(co_done, NT)
            for v in range(NV + LAG):
                if v + LEAD < NV:
                    scores(v + LEAD)
                if v < NV:
                    probs_t(v)
                if v >= LAG:
                    values(v - LAG)

            pe.wait_ge(p_done, NV)

            def project(half, u, t):
                n = SPLIT_NO[f"O{half}", u]
                wh, wl = slot_w(n, w_hi_sb), slot_w(n, w_lo_sb)
                for k in range(2):
                    c = (slice(None), K_ORDER[2 * u + k], slice(t * P, t * P + P))
                    mm = three(pe, ps[:, 4 * half + t, :], ht_hi[c], ht_lo[c], wh[:, k, :], wl[:, k, :],
                               u + k == 0, u == 3 and k == 1)
                return mm

            for u in range(4):
                pe.wait_ge(w_lo, SPLIT_NO["O0", u] + 1)
                if u == 2:
                    pe.wait_ge(ht_done, HTN["attn", NT - 1, 0] + 1)
                for t in range(NT):
                    mm = project(0, u, t)
                    if u == 3 and t < NT - 1:
                        mm.then_inc(y_done, 1)
                mm.then_inc(w_used, 1)
                if u == 0:
                    for t in range(NT - 1):
                        rows_t("attn", t)
                if u == 1:
                    rows_t("attn", NT - 1)
            for t in range(NT):
                for u in range(4):
                    pe.wait_ge(w_lo, SPLIT_NO["O1", u] + 1)
                    mm = project(1, u, t)
                    if t == NT - 1:
                        mm.then_inc(w_used, 1)
                if t < NT - 1:
                    mm.then_inc(y_done, 1)
                if t >= 1:
                    rows_t("ffn", t - 1)
            rows_t("ffn", NT - 1)

            pe.wait_ge(ht_done, len(HT))
            pe.wait_ge(resid, 2 * NT)
            with pe.Fori(0, NF // FR) as i:
                for j in range(FR):
                    pe.wait_ge(w_lo, i * FR + (NS + j + 1))
                    for k in range(NK):
                        c = slice(k * P, k * P + P)
                        mm = three(pe, ps[:, 4 + j, :], w_hi_sb[:, j, c], w_lo_sb[:, j, c], ht_hi[:, k, :],
                                   ht_lo[:, k, :], k == 0, k == NK - 1)
                    mm.then_inc(w_used, 1)

            def second(j, w_count, a_count, first=False, final_unit=False):
                pe.wait_ge(w_lo, w_count)
                pe.wait_ge(al_done, a_count)
                for t in range(NT):
                    if first and t == NT // 2:
                        pe.wait_ge(bank_free, NF)
                    rows = slice(t * P, t * P + P)
                    for b in range(2):
                        n = slice(b * 512, b * 512 + 512)
                        mm = three(pe, ps[:, 2 * t + b, :], a_hi[:, j % 2, rows], a_lo[:, j % 2, rows],
                                   w_hi_sb[:, j, n], w_lo_sb[:, j, n], first, final_unit)
                    if final_unit:
                        mm.then_inc(m_done, 1)
                if not final_unit:
                    mm.then_inc(w_used, 1)

            for j in range(FR):
                second(j, NS + NF + j + 1, j + 1, first=j == 0)
            with pe.Fori(1, NF // FR - 1) as i:
                for j in range(FR):
                    second(j, i * FR + (NS + NF + j + 1), i * FR + (j + 1))
            for j in range(FR):
                f = NF - FR + j
                second(j, NS + NF + f + 1, f + 1, final_unit=j == FR - 1)


def rope_tables():
    import numpy as np

    inv = np.float32(10000.0) ** (-np.arange(HALF, dtype=np.float32) / np.float32(HALF))
    ang = np.arange(SEQ, dtype=np.float32)[:, None] * inv[None, :]
    c, s = np.cos(ang), np.sin(ang)
    table = np.stack([np.concatenate([c, c], 1), np.concatenate([-s, s], 1)], 1).astype(np.float32)
    return table.reshape(NT, P, 2, HD).transpose(1, 0, 2, 3)


def layouts(i):
    import numpy as np

    w = i["w_in"][0]
    q_end = AW
    kv = {n: slice(q_end + k * P, q_end + (k + 1) * P) for k, n in
          enumerate(["kc", "vc", "k_sel", "v_sel", "k_win", "v_win"])}
    g0 = q_end + 6 * P
    zu, zv = slice(g0 + 3 * NH, g0 + 3 * NH + AW), slice(g0 + 3 * NH + AW, g0 + 3 * NH + 2 * AW)

    def units(a, order=range(NK)):
        return a.reshape(NK, P, -1)[list(order)].reshape(4, 2, P, -1).transpose(0, 2, 1, 3).reshape(4, P, -1)

    group = {"A": w[:, 0:AW], "B": w[:, slice(kv["k_sel"].start, kv["v_win"].stop)],
             "C": np.concatenate([w[:, g0:g0 + 3 * NH], w[:, kv["kc"]], w[:, kv["vc"]]], 1),
             "E": w[:, zv], "D": w[:, zu]}
    wo = i["w_out"][0]
    return {
        "x": i["x"][0].reshape(NT, P, D),
        "w512": np.concatenate([units(group[g]) for g in "ABED"]
                               + [units(wo[:, h * 512:h * 512 + 512], K_ORDER) for h in range(2)]),
        "w_c": units(group["C"]),
        "cmp_w1": i["cmp_w1"][0].reshape(2, 4, 4, P, CMP_HID).transpose(0, 1, 3, 2, 4).reshape(2, 4, P, UW),
        "cmp_w2": i["cmp_w2"][0].reshape(2, 2, P, HD).transpose(2, 0, 1, 3),
        "cmp_pe": i["cmp_pe"][0].reshape(2, 16, P).transpose(2, 0, 1),
        "sp_w": i["sp_w"][0].transpose(2, 0, 1),
        "sp_b": i["sp_b"][0].T,
        "g_rows": np.concatenate([i["g_mix_norm"], i["g_out"], i["g_ffn_norm"]], 0),
        "g_heads": np.concatenate([i["g_q"], i["g_k"][0, 1:3]], 0),
        "g_sgu": i["g_sgu"].reshape(1, NG * HD),
        "g_kc": np.concatenate([i["g_k"][0, 0], i["g_k"][0, 0]])[:, None],
        "rope": rope_tables(),
        "w_ff1": i["w_ff1"][0].reshape(NK, P, NF, P).transpose(2, 1, 0, 3).reshape(NF, P, D),
        "w_ff2": i["w_ff2"][0].reshape(NF, P, D),
    }


def kernel(**inputs):
    import numpy as np
    import concourse.bacc as bacc
    from concourse.bass_utils import run_bass_kernel_spmd

    nc = bacc.Bacc("TRN2", target_bir_lowering=False, num_devices=1)
    sent, args = {}, {}
    for name, a in layouts({k: np.asarray(v) for k, v in inputs.items()}).items():
        sent[f"in_{name}"] = np.ascontiguousarray(a)
        args[name] = nc.dram_tensor(f"in_{name}", a.shape, F32, kind="ExternalInput").ap()
    y = nc.dram_tensor("out_y", (NT, P, D), F32, kind="ExternalOutput").ap()
    hybrid_block(nc, **args, y=y)
    r = run_bass_kernel_spmd(nc, [sent], core_ids=[0])
    return r.results[0]["out_y"].reshape(1, SEQ, D)
```

```python
from contextlib import ExitStack

import concourse.bass as bass
from concourse import mybir

F32 = mybir.dt.float32
F32R = mybir.dt.float32r
BF16 = mybir.dt.bfloat16
ALU = mybir.AluOpType
ACT = mybir.ActivationFunctionType
AX = mybir.AxisListType

P = 128
SEQ, D = 512, 1024
NT = SEQ // P
NK = D // P
HD = 64
HALF = HD // 2
NH, NKV = 8, 2
GQA = NH // NKV
AW = NH * HD
NG = 8
NB = 2
CMP_STRIDE, CMP_BLOCK, CMP_HID = 16, 32, 256
NC = (SEQ - CMP_BLOCK) // CMP_STRIDE + 1
NCP = 32
FF = 4 * D
NF = FF // P
EPS = 1e-6
MASKED = -1e30
MAX_FLOOR = -1e20
SCALE = HD ** -0.5

UW = 1024
RAW = 4
HL = 6
FR = 4
CW = 3 * NH + 2 * P
K_ORDER = [4, 5, 6, 7, 0, 1, 2, 3]
STREAM = ([("split", g, u) for g in ["A", "B", "C", "E"] for u in range(4)]
          + [("split", "D", u) for u in range(2)]
          + [("direct", kv, u) for kv in range(2) for u in range(4)]
          + [("split", "D", u) for u in range(2, 4)]
          + [("split", f"O{h}", u) for h in range(2) for u in range(2)]
          + [("split", f"O{h}", u) for h in range(2) for u in range(2, 4)])
SPLITS = [i for i, s in enumerate(STREAM) if s[0] == "split"]
NS = len(SPLITS)
NW = NS - 8
SPLIT_NO = {STREAM[i][1:]: n for n, i in enumerate(SPLITS)}
FS = [(NS + j) % HL for j in range(FR)]
assert len(STREAM) % RAW == 0 and NF % FR == 0 and FR == RAW

NORMS = ([("x", t) for t in range(NT)] + [("mix", t) for t in range(NT)]
         + [("attn", 0), ("attn", 1), ("ffn", 0), ("attn", 2), ("ffn", 1), ("attn", 3), ("ffn", 2), ("ffn", 3)])
NORM = {n: i for i, n in enumerate(NORMS)}
KINDS = ["x", "mix", "attn", "ffn"]
HT = ([("x", t, i) for t in range(NT) for i in range(2)] + [("mix", t, 0) for t in range(NT)]
      + [("attn", 0, 0), ("attn", 1, 0), ("ffn", 0, 0), ("ffn", 0, 1), ("attn", 2, 0), ("attn", 3, 0),
         ("ffn", 2, 0), ("ffn", 1, 0), ("ffn", 1, 1), ("ffn", 3, 0), ("ffn", 2, 1), ("ffn", 3, 1)])
HTN = {k: n for n, k in enumerate(HT)}
ROWS = ([k for k in HT[:4 * NT] if k[0] != "x" or k[2] == 0]
        + [("attn", 2, 0), ("ffn", 1, 0), ("ffn", 1, 1), ("attn", 3, 0), ("ffn", 2, 0), ("ffn", 2, 1),
           ("ffn", 3, 0), ("ffn", 3, 1)])
ROWN = {k: n for n, k in enumerate(ROWS)}

SEQUENCE = [("x", 0), ("x", 1), ("out", "A", 0), ("x", 2), ("out", "A", 1), ("x", 3), ("out", "A", 2),
            ("out", "A", 3), ("out", "B", 0), ("q", 0), ("out", "B", 1), ("q", 1),
            ("out", "B", 2), ("q", 2), ("out", "B", 3), ("q", 3),
            ("gate",), ("k", 0), ("cmp_in", 0), ("k", 1), ("gateT",), ("cmp_in", 1), ("k", 2),
            ("out", "E", 0), ("k", 3), ("out", "E", 1), ("hid", 0), ("out", "E", 2), ("hidT", 0),
            ("hid", 1), ("kcmp",), ("out", "E", 3), ("hidT", 1), ("out", "D", 0), ("vcmp",), ("kcmpT",),
            ("out", "D", 1), ("cs", 0), ("cs", 1), ("sp", 0), ("sp", 1), ("sp", 2), ("sp", 3),
            ("out", "D", 2), ("mixT", 0), ("mixT", 1), ("out", "D", 3), ("cmpPT", 0), ("cmpPT", 1), ("s",),
            ("cmpO", 0), ("cmpO", 1), ("cmpO", 2), ("cmpO", 3), ("mixT", 2)]
FILLS = {"x": 2, "q": 3, "k": 2}
NOT_FILLS = ("out", "gate", "cmp_in", "s")
FILL = {}
for _s in SEQUENCE:
    for _i in range(0 if _s[0] in NOT_FILLS else FILLS.get(_s[0], 1)):
        FILL[(*_s, _i)] = len(FILL)
FILL_KEY = list(FILL)
OUTS = [s for s in SEQUENCE if s[0] in ("out", "gate", "cmp_in")]
OUT = {s: i for i, s in enumerate(OUTS)}
LAST_OUT = {("out", g, NT - 1): g for g in "ABED"}
LAST_OUT["cmp_in", 1] = "C"
OUT_NO = {s: n for n, s in enumerate(s for s in OUTS if s not in LAST_OUT)}

STEPS = [(t, h, b) for t in range(NT) for h in range(NH) for b in range(NB)]
NV = len(STEPS)
LEAD = 2
LAG = 2
WARM = 27
SBANKS = 3

PAIRED = NH * NB


def s_no(v):
    return v // 2 if v < PAIRED else v - PAIRED // 2


def s_before(v):
    return max((u for u in range(v) if s_no(u) == s_no(v) - SBANKS), default=None)


JB = 3
JOBS = {("mix", 3, 0): 1}
JOBS.update({("mixo", t, 0): 2 + 4 * t for t in range(NT)})
JOBS.update({("mixo", t, 1): 18 + 4 * t for t in range(NT)})
JOBS.update({("attn", 0, 0): 34, ("attno", 0, 0): 36, ("attn", 1, 0): 40, ("attno", 0, 1): 41, ("ffn", 0, 0): 45,
             ("attno", 1, 0): 46, ("ffn", 0, 1): 50, ("attno", 1, 1): 51, ("attn", 2, 0): 55,
             ("attno", 2, 0): 56})


def steps_of(k):
    return 4 if k[0] in ("mixo", "attno") else 1


CHUNKS = {v + c: (k, c) for k, v in JOBS.items() for c in range(steps_of(k))}
ENDS = {v + steps_of(k) - 1: k for k, v in JOBS.items()}
assert max(CHUNKS) < NV + LAG and len(CHUNKS) == sum(map(steps_of, JOBS))
TAIL = [("attno", 2, 1), ("attn", 3, 0), ("ffn", 2, 0), ("ffn", 1, 0), ("ffn", 1, 1), ("attno", 3, 0),
        ("attno", 3, 1), ("ffn", 3, 0), ("ffn", 2, 1), ("ffn", 3, 1)]
JOB_BANK = {k: JB for k in JOBS}
JOB_BANK.update({("ffn", 1, 0): 5, ("ffn", 1, 1): 6,
                 ("attno", 2, 1): 3, ("attn", 3, 0): 0, ("ffn", 2, 0): 4, ("ffn", 2, 1): 3, ("attno", 3, 0): 1,
                 ("attno", 3, 1): 2, ("ffn", 3, 0): 0, ("ffn", 3, 1): 1})
JOB = {k: n for n, k in enumerate(list(JOBS) + TAIL)}
JOB_KEY = list(JOB)
ADDS = [k for k in JOB if k[0] in ("mixo", "attno")]
ADD_NO = {k: n for n, k in enumerate(ADDS)}


def hybrid_block(nc, x, w512, w_c, cmp_w1, cmp_w2, cmp_pe, sp_w, sp_b, g_rows, g_heads, g_sgu,
                 g_kc, rope, w_ff1, w_ff2, y):
    ctx = ExitStack()
    with ctx:
        top = [nc.sbuf_base]

        def at(name, shape, dt, offset):
            return nc.alloc_sbuf_tensor_at(name, shape, dt, offset=offset)

        def area(size):
            o = (top[0] + 31) // 32 * 32
            top[0] = o + size
            assert top[0] <= nc.sbuf_usable_end, (top[0], nc.sbuf_usable_end)
            return o

        def sb(name, shape, dt=F32):
            n = 1
            for s in shape[1:]:
                n *= s
            return at(name, shape, dt, area(n * (2 if dt == BF16 else 4)))

        raw = sb("raw", [P, RAW, UW])
        w_hi_sb = sb("w_hi_sb", [P, HL, UW], F32R)
        w_lo_sb = sb("w_lo_sb", [P, HL, UW], F32R)
        o_ht = [area(NK * SEQ * 4), area(NK * SEQ * 4)]
        ht_hi = at("ht_hi", [P, NK, SEQ], F32R, o_ht[0])
        ht_lo = at("ht_lo", [P, NK, SEQ], F32R, o_ht[1])
        o_x = area(NT * D * 4)
        xs = at("xs", [P, NT, D], F32, o_x)
        o_o = area(NT * D * 4)
        o_sb = at("o_sb", [P, NT, D], F32, o_o)
        eps_sb = sb("eps_sb", [P, 1])

        ident = sb("ident", [P, P])
        ident16 = sb("ident16", [P, P], BF16)
        causal16 = sb("causal16", [P, NB, P], BF16)
        cmp_mask = sb("cmp_mask", [P, NT, NCP])
        spb_sb = sb("spb_sb", [P, NG])
        gkc_sb = sb("gkc_sb", [P, 1])
        glog = sb("glog", [P, NT, 3 * NH])
        ssq = sb("ssq", [P, len(NORMS)])
        rstd = sb("rstd", [P, len(NORMS)])
        hss = sb("hss", [P, 3, NT, NG])
        hrs = sb("hrs", [P, 3, NT, NG])
        ksum = sb("ksum", [P, 2])
        nmax = sb("nmax", [P, NV])
        psum_p = sb("psum_p", [P, NT, NH, NB])
        coef = sb("coef", [P, NT, NH, NB])
        cmx = sb("cmx", [P, NT * NH])
        ccf = sb("ccf", [P, NT * NH])

        o_r = area(0)
        rest = nc.sbuf_usable_end - o_r
        top[0] = o_r
        qT = sb("qT", [P, NH, SEQ], F32R)
        kT = sb("kT", [P, NB, NKV, 2, SEQ], F32R)
        o_qcT = area(NH // 2 * SEQ * 4)
        qcT = at("qcT", [P, NH // 2, SEQ], F32, o_qcT)
        v_sb = sb("v_sb", [P, NT, NB, NKV * HD])
        o_t = area(18 * 1024)
        t1 = at("t1", [P, 512], F32, o_t)
        t2 = at("t2", [P, 512], F32, o_t + 2048)
        zk = at("zk", [P, NT, 256], F32, o_t + 4096)
        sqk = at("sqk", [P, 2, 256], F32, o_t + 8192)
        stack = at("stack", [P, 2, NH, 2, HD], F32, o_t + 10240)
        p_sb = at("p_sb", [P, 3, SEQ], F32, o_t)
        pt_sb = at("pt_sb", [P, 3, SEQ], F32, o_t + 3 * 2048)
        gh_sb = sb("gh_sb", [P, 3, HD])
        o_gsgu = area(D * 4)
        gsgu_sb = at("gsgu_sb", [P, NG * HD], F32, o_gsgu)
        rope_sb = at("rope_sb", [P, NT, 2, HD], F32, o_gsgu + NG * HD * 4)
        grow = sb("grow", [P, D])
        tmp = at("tmp", [P, 2, 512], F32, o_t + 7 * 2048)
        grow_ffn = at("grow_ffn", [P, D], F32, o_gsgu)
        scr = at("scr", [P, D], F32, o_qcT)
        assert NF * SEQ * 4 <= rest
        act_sb = at("act_sb", [P, NF, SEQ], F32, o_r)
        a_hi = at("a_hi", [P, 2, SEQ], F32R, o_o)
        a_lo = at("a_lo", [P, 2, SEQ], F32R, o_o + 2 * SEQ * 4)

        par = at("par", [P, 2, NKV, SEQ // 2], F32, o_x)
        blk = at("blk", [P, 2, 16, NKV, NC], F32, o_x + 4096)
        spw_sb = at("spw_sb", [P, NG, P], F32, o_x + 12288)
        cw2_sb = sb("cw2_sb", [P, 2, 2, HD])
        pe_sb = sb("pe_sb", [P, 2, 16])
        gate_t = at("gate_t", [3 * NH, SEQ], F32, o_o + 3 * D * 4 + 2048)
        pc = at("pc", [P, NT, NKV, GQA, NCP], F32, o_t + 4096)
        pcT = at("pcT", [P, NT * NKV, P], F32, o_t + 8192)
        hid = at("hid", [NKV * NC, 2, CMP_HID], F32, o_t + 8192)
        vblk = at("vblk", [P, NKV, GQA * HD], F32, o_t + 12288)
        kn = at("kn", [NKV * NCP, 2, HD], F32, o_t + 14336)
        kcT = at("kcT", [P, NKV, 2, NCP], F32, o_t + 14848)
        ksq = at("ksq", [NKV * NCP, HD], F32, o_t + 15360)
        hid_k = at("hid_k", [P, 2, NKV, NCP], F32, o_t + 15616)
        hid_v = at("hid_v", [P, 2, NKV, GQA, NCP], F32, o_t + 16128)

        ps = ctx.enter_context(nc.psum_tensor("ps", [P, 8, 512], F32))

        def sem(name):
            return ctx.enter_context(nc.semaphore(name))

        raw_in = [sem(f"raw_in{i}") for i in range(RAW)]
        w_hi, w_lo = sem("w_hi"), sem("w_lo")
        w_used = sem("w_used")
        cw_used = sem("cw_used")
        x_in = [sem(f"x_in{t}") for t in range(NT)]
        x_again = [sem(f"x_again{t}") for t in range(NT)]
        grow_in, grow_out_in, grow_ffn_in = sem("grow_in"), sem("grow_out_in"), sem("grow_ffn_in")
        tables_in, spat_in = sem("tables_in"), sem("spat_in")
        y_out = sem("y_out")
        eps_made, ident_made, masks_made = sem("eps_made"), sem("ident_made"), sem("masks_made")
        spw_made, pads_made = sem("spw_made"), sem("pads_made")
        n_ssq, n_root, n_rstd, n_rows = [sem(f"n_{k}") for k in ("ssq", "root", "rstd", "rows")]
        ht_half, ht_done = sem("ht_half"), sem("ht_done")
        filled = sem("filled")
        free = [sem(f"free{b}") for b in range(4)]
        out_done, out_evac = sem("out_done"), sem("out_evac")
        h_ssq, h_sum, h_root, h_step = [sem(f"h_{k}") for k in ("ssq", "sum", "root", "step")]
        rot, st_hi, st_lo = sem("rot"), sem("st_hi"), sem("st_lo")
        blk_done = sem("blk_done")
        zv_sq, zv_sum, zv_norm = sem("zv_sq"), sem("zv_sum"), sem("zv_norm")
        sv_done, mixed = sem("sv_done"), sem("mixed")
        kc_sq, kc_root, kc_rstd = [sem(f"kc_{k}") for k in ("sq", "root", "rstd")]
        cs_step, c_exp = sem("cs_step"), sem("c_exp")
        c_step, c_probs = sem("c_step"), sem("c_probs")
        g_exp, g_step = sem("g_exp"), sem("g_step")
        co_done = [sem("co_done_early"), sem("co_done_late")]
        s_done, s_max, p_done = sem("s_done"), sem("s_max"), sem("p_done")
        pt_done = sem("pt_done")
        pt_evac = [sem("pt_evac_sel"), sem("pt_evac_win")]
        pv_done = sem("pv_done")
        o_step, o_evac = sem("o_step"), sem("o_evac")
        job_done, added = sem("job_done"), sem("added")
        r2_step = sem("r2_step")
        bank_free = sem("bank_free")
        squared = sem("squared")
        ah_done, al_done = sem("ah_done"), sem("al_done")
        m_done, final = sem("m_done"), sem("final")

        block = ctx.enter_context(nc.Block())

        def slot_w(n, halves, size=512):
            return halves[:, n % HL, 0:2 * size].rearrange("p (k n) -> p k n", k=2)

        def three(pe, out, l_hi, l_lo, r_hi, r_lo, start, stop):
            pe.matmul(out, l_hi, r_hi, start=start, stop=False)
            pe.matmul(out, l_hi, r_lo, start=False, stop=False)
            return pe.matmul(out, l_lo, r_hi, start=False, stop=stop)

        def fill_bank(j):
            return 4 + j % 4

        def wait_free(eng, j):
            key = FILL_KEY[j]
            if key[0] in ("x", "mixT"):
                eng.wait_ge(ht_done, HTN["x" if key[0] == "x" else "mix", key[1], key[2]] + 1)
            elif key[0] == "cmpO":
                eng.wait_ge(co_done[key[1] // 2], key[1] % 2 + 1)
            else:
                eng.wait_ge(free[j % 4], sum(FILL_KEY[i][0] not in ("x", "mixT", "cmpO")
                                             for i in range(j % 4, j + 1, 4)))

        def wait_bank(eng, j):
            if j >= 4:
                wait_free(eng, j - 4)

        def wait_fill(eng, j):
            eng.wait_ge(filled, j + 1)

        def wait_used(eng, n):
            if n < NW:
                eng.wait_ge(w_used, n + 1)
            else:
                kind, half = ("mixo" if n < NW + 4 else "attno"), (n - NW) % 4 // 2
                eng.wait_ge(job_done, JOB[kind, NT - 1, half] + 1)

        def job_taken(eng, k):
            if k in ADD_NO:
                eng.wait_ge(added, ADD_NO[k] + 1)
            else:
                eng.wait_ge(ht_done, HTN[k] + 1)

        def wait_out(eng, s):
            if s in LAST_OUT:
                eng.wait_ge(w_used, SPLIT_NO[LAST_OUT[s], 3] + 1)
            else:
                eng.wait_ge(out_done, OUT_NO[s] + 1)

        def bc(ap, shape):
            return ap.broadcast_to(shape)

        @block.sync
        def _(sp):
            groups = ["A", "B", "E", "D", "O0", "O1"]

            def load(i):
                kind, g, u = STREAM[i]
                if i >= RAW:
                    was = STREAM[i - RAW]
                    if was[0] == "split":
                        sp.wait_ge(w_lo, SPLIT_NO[was[1:]] + 1)
                    elif was[2] < 3:
                        sp.wait_ge(cw_used, 3 * was[1] + was[2] + 1)
                    else:
                        sp.wait_ge(filled, FILL["hid", was[1], 0] + 1)
                if kind == "direct":
                    src, n = cmp_w1[g, u], UW
                elif g == "C":
                    src, n = w_c[u], 2 * CW
                else:
                    src, n = w512[4 * groups.index(g) + u], UW
                sp.dma_start(raw[:, i % RAW, 0:n], src).then_inc(raw_in[i % RAW], 16)

            for i in range(RAW):
                if i in (0, 2):
                    sp.dma_start(xs[:, i // 2, :], x[i // 2]).then_inc(x_in[i // 2], 16)
                if i == 0:
                    sp.dma_start(grow[:, :], g_rows[0:1, :].broadcast_to([P, D])).then_inc(grow_in, 16)
                load(i)
            for t in range(2, NT):
                sp.dma_start(xs[:, t, :], x[t]).then_inc(x_in[t], 16)
            for i in range(RAW, len(STREAM)):
                if STREAM[i] == ("split", "O0", 2):
                    sp.wait_ge(filled, FILL["sp", 3, 0] + 1)
                    for t in range(NT):
                        sp.dma_start(xs[:, t, :], x[t]).then_inc(x_again[t], 16)
                load(i)
            with sp.Fori(0, NF // RAW) as i:
                for j in range(RAW):
                    sp.wait_ge(w_lo, i * RAW + (NS + j - RAW + 1))
                    sp.dma_start(raw[:, j, :], w_ff1[i * RAW + j]).then_inc(raw_in[j], 16)
            with sp.Fori(0, NF // RAW) as i:
                for j in range(RAW):
                    sp.wait_ge(w_lo, i * RAW + (NS + NF + j - RAW + 1))
                    sp.dma_start(raw[:, j, :], w_ff2[i * RAW + j]).then_inc(raw_in[j], 16)
            for t in range(NT - 1):
                sp.wait_ge(final, t + 1)
                sp.dma_start(y[t], xs[:, t, :]).then_inc(y_out, 16)
            for b in range(2):
                c = slice(b * 512, b * 512 + 512)
                sp.wait_ge(final, NT + b)
                sp.dma_start(y[NT - 1, :, c], xs[:, NT - 1, c]).then_inc(y_out, 16)
            sp.wait_ge(y_out, 16 * (NT + 1))

        @block.gpsimd
        def _(pool):
            pool.memset(eps_sb[:, :], EPS).then_inc(eps_made, 1)
            pool.memset(ident[:, :], 0.0).then_inc(ident_made, 1)
            pool.wait_ge(ident_made, 1)
            pool.affine_select(out=ident[:, :], in_=ident[:, :], compare_op=ALU.not_equal, fill=1.0,
                               base=0, pattern=[[-1, P]], channel_multiplier=1).then_inc(ident_made, 1)
            pool.dma_start(gh_sb[:, :, :], g_heads[:, :].unsqueeze(0).broadcast_to([P, 3, HD])
                           ).then_inc(tables_in, 16)
            pool.dma_start(rope_sb[:, :, :, :], rope[:, :, :, :]).then_inc(tables_in, 16)
            pool.dma_start(gsgu_sb[:, :], g_sgu[0:1, :].broadcast_to([P, NG * HD])).then_inc(tables_in, 16)
            pool.dma_start(spb_sb[:, :], sp_b[:, :]).then_inc(tables_in, 16)
            pool.dma_start(gkc_sb[:, :], g_kc[:, :]).then_inc(tables_in, 16)
            pool.dma_start(cw2_sb[:, :, :, :], cmp_w2[:, :, :, :]).then_inc(tables_in, 16)
            pool.dma_start(pe_sb[:, :, :], cmp_pe[:, :, :]).then_inc(tables_in, 16)
            pool.memset(ident16[:, :], 0.0).then_inc(masks_made, 1)
            pool.memset(causal16[:, :, :], 0.0).then_inc(masks_made, 1)
            pool.memset(cmp_mask[:, :, :], 0.0).then_inc(masks_made, 1)
            pool.wait_ge(masks_made, 3)
            pool.affine_select(out=ident16[:, :], in_=ident16[:, :], compare_op=ALU.not_equal, fill=1.0,
                               base=0, pattern=[[-1, P]], channel_multiplier=1).then_inc(masks_made, 1)
            pool.affine_select(out=causal16[:, :, :], in_=causal16[:, :, :], compare_op=ALU.is_ge, fill=MASKED,
                               base=0, pattern=[[0, NB], [-1, P]], channel_multiplier=1).then_inc(masks_made, 1)
            pool.affine_select(out=cmp_mask[:, :, :], in_=cmp_mask[:, :, :], compare_op=ALU.is_ge,
                               fill=MASKED, base=1 - CMP_BLOCK, pattern=[[P, NT], [-CMP_STRIDE, NCP]],
                               channel_multiplier=1).then_inc(masks_made, 1)
            pool.wait_ge(filled, FILL["x", NT - 1, 1] + 1)
            pool.dma_start(spw_sb[:, :, :], sp_w[:, :, :]).then_inc(spat_in, 16)
            pool.wait_ge(spat_in, 16)
            pool.affine_select(out=spw_sb[:, :, :], in_=spw_sb[:, :, :], compare_op=ALU.is_ge, fill=0.0,
                               base=0, pattern=[[0, NG], [1, P]], channel_multiplier=-1).then_inc(spw_made, 1)
            pool.wait_ge(filled, FILL["k", NT - 1, 1] + 1)
            pool.memset(vblk[:, :, :], 0.0).then_inc(pads_made, 1)
            pool.memset(kcT[:, :, :, :], 0.0).then_inc(pads_made, 1)
            pool.memset(hid_k[:, :, :, :], 0.0).then_inc(pads_made, 1)
            pool.memset(hid_v[:, :, :, :, :], 0.0).then_inc(pads_made, 1)
            pool.wait_ge(n_rows, NT)
            pool.dma_start(grow[:, :], g_rows[1:2, :].broadcast_to([P, D])).then_inc(grow_out_in, 16)
            pool.wait_ge(zv_norm, NT)
            pool.dma_start(grow_ffn[:, :], g_rows[2:3, :].broadcast_to([P, D])).then_inc(grow_ffn_in, 16)

        MASKS, PADS = 6, 4

        def norm_src(kind, t):
            if kind in ("x", "ffn"):
                return xs[:, t, :]
            return o_sb[:, t, AW:] if kind == "mix" else o_sb[:, t, 0:AW]

        def norm_dst(kind, t, cols):
            if kind in ("x", "ffn"):
                return (xs if kind == "x" else o_sb)[:, t, cols]
            return o_sb[:, t, AW:]

        def stat(m, kind, t, n=1):
            c = KINDS.index(kind) * NT + t
            return m[:, c:c + n]

        def norm_width(kind):
            return D if kind in ("x", "ffn") else AW

        def halves_of(kind, t, i, fill):
            k0 = {"x": 4 * i, "ffn": 4 * i, "mix": 4, "attn": 0}[kind]
            src = ps[:, fill, :].rearrange("p (k s) -> p k s", k=4)
            cut = (slice(None), slice(k0, k0 + 4), slice(t * P, t * P + P))
            return src, ht_hi[cut], ht_lo[cut]

        def ht_bank(kind, t, i):
            if kind == "x":
                return fill_bank(FILL["x", t, i])
            if ("mixT", t, 0) in FILL and kind == "mix":
                return fill_bank(FILL["mixT", t, 0])
            return JOB_BANK[kind, t, i]

        def kstack(m, w):
            return stack[:, m % 2, :, :, :].rearrange("p h e d -> p (h e d)").rearrange(
                "p (c w e d) -> p c w e d", c=NB * NKV, w=2, e=2)[:, :, w, :, :]

        def k_dup():
            k = t1[:, 0:256].rearrange("p (c d) -> p c d", d=HD)
            return bc(k.unsqueeze(2), [P, NB * NKV, 2, HD])

        def stack_read(m):
            return FILL[("q", m, 1) if m < NT else ("k", m - NT, 1)]

        @block.scalar
        def _(act):
            def hi(n, width=UW):
                i = SPLITS[n]
                act.wait_ge(raw_in[i % RAW], 16 * (i // RAW + 1))
                if n >= HL:
                    wait_used(act, n - HL)
                act.activation(w_hi_sb[:, n % HL, 0:width], raw[:, i % RAW, 0:width], ACT.Copy
                               ).then_inc(w_hi, 1)

            def norm_sum(kind, t, scratch):
                j = NORM[kind, t]
                if j:
                    act.wait_ge(n_ssq, j)
                act.activation(scratch, norm_src(kind, t), ACT.Square, accum_out=stat(ssq, kind, t)
                               ).then_inc(n_ssq, 1)

            def norm_root(kind, t, n=1):
                act.wait_ge(n_ssq, NORM[kind, t + n - 1] + 1)
                act.activation(stat(rstd, kind, t, n), stat(ssq, kind, t, n), ACT.Sqrt, bias=eps_sb[:, :],
                               scale=1.0 / norm_width(kind)).then_inc(n_root, 1)

            def ht_hi_evac(kind, t, i):
                if (kind, t, i) not in JOB:
                    act.wait_ge(filled, FILL["x" if kind == "x" else "mixT", t, i] + 1)
                else:
                    act.wait_ge(job_done, JOB[kind, t, i] + 1)
                src, h, _ = halves_of(kind, t, i, ht_bank(kind, t, i))
                act.activation(h, src, ACT.Copy).then_inc(ht_half, 1)

            act.wait_ge(eps_made, 1)
            act.activation(rstd[:, 4 * NT - 1:4 * NT], eps_sb[:, :], ACT.Sqrt)

            def stats_root(which, t):
                c = which * NT + t + 1
                act.wait_ge(h_sum, c)
                n = NH if which == 0 else NB * NKV
                act.activation(hrs[:, which, t, 0:n], hss[:, which, t, 0:n], ACT.Sqrt,
                               bias=eps_sb[:, :], scale=1.0 / HD).then_inc(h_root, 1)

            def evac_q(t):
                o = OUT["out", "A", t]
                wait_out(act, ("out", "A", t))
                act.activation(o_sb[:, t, AW:], ps[:, o % 4, :], ACT.Square).then_inc(h_ssq, 1)
                act.activation(o_sb[:, t, 0:AW], ps[:, o % 4, :], ACT.Copy).then_inc(out_evac, 1)

            def evac_kv(t):
                o = OUT["out", "B", t]
                src = ps[:, o % 4, :].rearrange("p (b w n) -> p b w n", b=NB, w=2)
                wait_out(act, ("out", "B", t))
                if t >= 2:
                    act.wait_ge(h_sum, NT + t - 1)
                act.activation(sqk[:, t % 2, :].rearrange("p (b n) -> p b n", b=NB), src[:, :, 0, :],
                               ACT.Square).then_inc(h_ssq, 1)
                act.activation(zk[:, t, :].rearrange("p (b n) -> p b n", b=NB), src[:, :, 0, :], ACT.Copy)
                act.activation(v_sb[:, t, :, :], src[:, :, 1, :], ACT.Copy).then_inc(out_evac, 1)

            def stack_hi(m):
                act.wait_ge(rot, m + 1)
                if m >= 2:
                    wait_fill(act, stack_read(m - 2))
                if m < NT:
                    act.activation(stack[:, m % 2, :, 0, :].bitcast(F32R),
                                   t1[:, :].rearrange("p (h d) -> p h d", h=NH), ACT.Copy).then_inc(st_hi, 1)
                else:
                    act.activation(kstack(m, 0).bitcast(F32R), k_dup(), ACT.Copy).then_inc(st_hi, 1)

            def fill_evac(key, i, dst, scale=1.0):
                j = FILL[(*key, i)]
                wait_fill(act, j)
                act.activation(dst, ps[:, fill_bank(j), :].rearrange("p (h s) -> p h s", h=dst.shape[1]),
                               ACT.Copy, scale=scale).then_inc(free[j % 4], 1)

            def q_evac(t):
                s = slice(t * P, t * P + P)
                fill_evac(("q", t), 0, qT[:, 0:4, s], SCALE)
                fill_evac(("q", t), 1, qT[:, 4:8, s], SCALE)
                fill_evac(("q", t), 2, qcT[:, :, s])

            def k_evac(t):
                for b in range(NB):
                    fill_evac(("k", t), b, kT[:, b, :, :, t * P:t * P + P].rearrange("p g w s -> p (g w) s"))

            def x_norm(t):
                act.wait_ge(x_in[t], 16)
                norm_sum("x", t, o_sb[:, NT - 1, :])
                norm_root("x", t)

            def x_hi(t):
                ht_hi_evac("x", t, 0)
                ht_hi_evac("x", t, 1)

            x_norm(0)
            hi(0)
            x_hi(0)
            hi(1)
            hi(2)
            x_norm(1)
            hi(3)
            x_norm(2)
            x_hi(1)
            x_norm(3)
            hi(4)
            x_hi(2)
            hi(5)
            evac_q(0)
            stats_root(0, 0)
            x_hi(3)
            stack_hi(0)
            evac_q(1)
            stats_root(0, 1)
            hi(6)
            hi(7)
            stack_hi(1)
            evac_q(2)
            stats_root(0, 2)
            evac_q(3)
            evac_kv(0)
            q_evac(0)
            stack_hi(2)
            stats_root(0, 3)
            hi(8, 2 * CW)
            evac_kv(1)
            q_evac(1)
            stack_hi(3)
            stats_root(1, 0)
            hi(9, 2 * CW)
            evac_kv(2)
            q_evac(2)
            stack_hi(4)
            stats_root(1, 1)
            hi(10, 2 * CW)
            hi(11, 2 * CW)
            evac_kv(3)
            q_evac(3)
            stack_hi(5)
            stats_root(1, 2)
            o = OUT["gate",]
            wait_out(act, ("gate",))
            act.activation(gate_t[:, :], ps[0:3 * NH, o % 4, :], ACT.Copy).then_inc(out_evac, 1)
            hi(12)
            hi(13)
            k_evac(0)
            stack_hi(6)
            stats_root(1, 3)

            def evac_cmp_in(kv):
                o = OUT["cmp_in", kv]
                wait_out(act, ("cmp_in", kv))
                for g in range(NKV):
                    for odd in range(2):
                        last = act.activation(par[HD * odd:HD * odd + HD, kv, g, :],
                                              ps[HD * g:HD * g + HD, o % 4, odd::2], ACT.Copy)
                last.then_inc(out_evac, 1)

            evac_cmp_in(0)
            k_evac(1)
            stack_hi(7)
            j = FILL["gateT", 0]
            wait_fill(act, j)
            act.activation(glog[:, :, :], ps[:, fill_bank(j), 0:NT * 3 * NH].rearrange("p (t c) -> p t c", t=NT),
                           ACT.Copy).then_inc(free[j % 4], 1)
            hi(14)
            hi(15)
            evac_cmp_in(1)
            k_evac(2)
            hi(16)
            hi(17)

            def evac_gelu(g, t):
                o = OUT["out", g, t]
                wait_out(act, ("out", g, t))
                dst = o_sb[:, t, 0:AW] if g == "E" else o_sb[:, t, AW:]
                act.activation(dst, ps[:, o % 4, :], ACT.Gelu_apprx_tanh).then_inc(out_evac, 1)

            def evac_hid(kv):
                j = FILL["hid", kv, 0]
                wait_fill(act, j)
                act.activation(hid[:, kv, :], ps[0:NKV * NC, fill_bank(j), 0:CMP_HID], ACT.Gelu_apprx_tanh
                               ).then_inc(free[j % 4], 1)

            def evac_hid_t(kv):
                j = FILL["hidT", kv, 0]
                wait_fill(act, j)
                act.wait_ge(pads_made, PADS)
                src = ps[:, fill_bank(j), 0:256].rearrange("p (f m) -> p f m", f=2)
                for half in range(2):
                    rows = src[:, half, 0:NKV * NC].rearrange("p (g n) -> p g n", g=NKV)
                    if kv == 0:
                        last = act.activation(hid_k[:, half, :, 0:NC], rows, ACT.Copy)
                    else:
                        last = act.activation(hid_v[:, half, :, :, 0:NC], bc(rows.unsqueeze(2), [P, NKV, GQA, NC]),
                                              ACT.Copy)
                last.then_inc(free[j % 4], 1)

            def zv_square(t):
                act.wait_ge(out_evac, OUT["out", "E", t] + 1)
                act.wait_ge(st_lo, 2 * NT)
                if t >= 2:
                    act.wait_ge(zv_sum, t - 1)
                act.activation((t1, t2)[t % 2][:, :], o_sb[:, t, 0:AW], ACT.Square).then_inc(zv_sq, 1)

            evac_gelu("E", 0)
            k_evac(3)
            zv_square(0)
            evac_gelu("E", 1)
            zv_square(1)
            evac_hid(0)
            evac_gelu("E", 2)
            zv_square(2)
            evac_hid_t(0)
            evac_hid(1)
            hi(18)
            hi(19)
            evac_gelu("E", 3)
            zv_square(3)
            evac_hid_t(1)
            j = FILL["kcmp", 0]
            wait_fill(act, j)
            act.activation(ksq[:, :], ps[0:NKV * NCP, fill_bank(j), 0:HD], ACT.Square,
                           accum_out=ksum[0:NKV * NCP, 0:1]).then_inc(kc_sq, 1)
            act.wait_ge(kc_sq, 1)
            act.activation(ksum[0:NKV * NCP, 1:2], ksum[0:NKV * NCP, 0:1], ACT.Sqrt,
                           bias=eps_sb[0:NKV * NCP, :], scale=1.0 / HD).then_inc(kc_root, 1)
            act.wait_ge(zv_sum, NT)
            act.activation(hrs[:, 2, :, :], hss[:, 2, :, :], ACT.Sqrt, bias=eps_sb[:, :], scale=1.0 / HD
                           ).then_inc(h_root, 1)
            evac_gelu("D", 0)
            j = FILL["kcmpT", 0]
            wait_fill(act, j)
            for e in range(2):
                rows = slice(HD * e, HD * e + HD)
                last = act.activation(kcT[rows, :, e, :], ps[rows, fill_bank(j), 0:NKV * NCP].rearrange(
                    "p (g n) -> p g n", g=NKV), ACT.Copy, scale=gkc_sb[rows, :])
            last.then_inc(free[j % 4], 1)
            hi(20)
            hi(21)
            evac_gelu("D", 1)
            wait_free(act, FILL["gateT", 0])
            act.activation(glog[:, :, :], glog[:, :, :], ACT.Exp, scale=-1.0).then_inc(g_exp, 1)
            act.wait_ge(cs_step, 3)
            act.activation(pc[:, :, :, :, :], pc[:, :, :, :, :], ACT.Exp, scale=SCALE).then_inc(c_exp, 1)
            evac_gelu("D", 2)
            for t in range(2):
                act.wait_ge(mixed, t + 1)
                norm_sum("mix", t, (t1, t2)[t % 2][:, :])
            act.wait_ge(mixed, 3)
            norm_sum("mix", 2, t1[:, :])
            ht_hi_evac("mix", 0, 0)
            ht_hi_evac("mix", 1, 0)
            evac_gelu("D", 3)

            def pct_evac(i):
                j = FILL["cmpPT", i, 0]
                wait_fill(act, j)
                act.activation(pcT[:, 4 * i:4 * i + 4, :], ps[:, fill_bank(j), :].rearrange("p (i s) -> p i s", i=4),
                               ACT.Copy).then_inc(free[j % 4], 1)

            def c_evac(i):
                j = FILL["cmpO", i, 0]
                wait_fill(act, j)
                act.wait_ge(mixed, i + 1)
                act.activation(o_sb[:, i, 0:AW], ps[:, fill_bank(j), :], ACT.Copy).then_inc(co_done[1], 1)

            pct_evac(0)
            pct_evac(1)
            act.wait_ge(mixed, 4)
            norm_sum("mix", 3, t2[:, :])
            norm_root("mix", 0, NT)
            IN0 = 16 * (len(STREAM) // RAW)

            def f_hi(slot, count, used=None):
                act.wait_ge(raw_in[slot], count)
                if used is None:
                    wait_used(act, NS - HL + slot)
                else:
                    act.wait_ge(w_used, used)
                act.activation(w_hi_sb[:, FS[slot], :], raw[:, slot, :], ACT.Copy).then_inc(w_hi, 1)

            def exp(v):
                t, h, b = STEPS[v]
                n = P * (t + 1)
                act.wait_ge(s_max, s_no(v) + 1)
                c = v % 2 * P if v < PAIRED else 0
                if v >= 3:
                    act.wait_ge(pt_done, v - 2)
                elif v == 2:
                    act.wait_ge(filled, FILL["cmpPT", 1, 0] + 1)
                act.activation(p_sb[:, v % 3, 0:n], ps[:, s_no(v) % SBANKS, c:c + n], ACT.Exp, bias=nmax[:, v:v + 1],
                               accum_out=psum_p[:, t, h, b:b + 1]).then_inc(p_done, 1)

            def pt(v):
                n = P * (STEPS[v][0] + 1)
                act.wait_ge(pt_done, v + 1)
                if v >= 3:
                    act.wait_ge(pv_done, v - 2)
                act.activation(pt_sb[:, v % 3, 0:n], ps[:, 4 + v % 2, 0:n], ACT.Copy).then_inc(pt_evac[1], 1)

            def job_act(k):
                if k in HTN:
                    ht_hi_evac(*k)

            exp(0)
            exp(1)
            c_evac(2)
            c_evac(3)
            for w in range(2, NV + LEAD + LAG):
                s = w - LEAD
                job_act(ENDS.get(s))
                if w < NV:
                    exp(w)
                if 0 <= s < NV and s % 2 == 1:
                    pt(s)
                if w == 2:
                    ht_hi_evac("mix", 2, 0)
                if s == 2:
                    hi(22)
                if s == 10:
                    hi(23)
                if s in (19, 22, 26, 28):
                    hi(24 + (19, 22, 26, 28).index(s))
                if s in (19, 35, 51):
                    act.wait_ge(o_evac, 2 * (s // 16))
                    norm_sum("attn", s // 16 - 1, scr[:, 0:AW])
                if s == 35:
                    norm_root("attn", 0, 2)
                if s == 51:
                    norm_root("attn", 2)
                if s in (42, 47):
                    f_hi((s - 42) // 5, IN0 + 16)
                if s in (48, 58):
                    t = (s - 48) // 10
                    act.wait_ge(added, ADD_NO["attno", t, 1] + 1)
                    norm_sum("ffn", t, scr[:, :])
            act.wait_ge(o_evac, 2 * NT)
            norm_sum("attn", 3, scr[:, 0:AW])
            ht_hi_evac("attn", 3, 0)
            ht_hi_evac("ffn", 2, 0)
            ht_hi_evac("ffn", 1, 0)
            ht_hi_evac("ffn", 1, 1)
            norm_root("attn", 3)
            act.wait_ge(added, ADD_NO["attno", 2, 1] + 1)
            norm_sum("ffn", 2, scr[:, :])

            ht_hi_evac("ffn", 3, 0)
            ht_hi_evac("ffn", 2, 1)
            f_hi(2, IN0 + 16)
            ht_hi_evac("ffn", 3, 1)
            f_hi(3, IN0 + 16)
            act.wait_ge(added, len(ADDS))
            norm_sum("ffn", 3, scr[:, :])

            def relu(f):
                i, j = f
                act.wait_ge(w_used, i * FR + (NW + j + 1))
                act.activation(act_sb[:, i * FR + j, :], ps[:, 4 + j, :], ACT.Relu).then_inc(bank_free, 1)

            with act.Fori(0, NF // FR - 1) as i:
                for j in range(FR):
                    relu((i, j))
                    f_hi(j, i * 16 + (IN0 + 32), i * FR + (NW + j + 1))

            IN1 = IN0 + 16 * (NF // RAW)

            def a_half(slot, f, used, squares):
                act.wait_ge(w_used, used)
                act.wait_ge(squared, squares)
                act.activation(a_hi[:, slot, :], act_sb[:, f, :], ACT.Copy).then_inc(ah_done, 1)

            for j in range(FR):
                relu((NF // FR - 1, j))
                f_hi(j, IN1 + 16, NW + NF - FR + j + 1)
                if j < 2:
                    a_half(j, j, NW + NF - FR, j + 1)
            with act.Fori(0, NF // FR - 1) as i:
                for j in range(FR):
                    a_half(j % 2, i * FR + (j + 2), i * FR + (NW + NF + j + 1), i * FR + (j + 3))
                    f_hi(j, i * 16 + (IN1 + 32), i * FR + (NW + NF + j + 1))
            for f in (NF - 2, NF - 1):
                a_half(f % 2, f, NW + NF + f - 1, f + 1)

        @block.vector
        def _(dve):
            def lo(n, width=UW):
                i = SPLITS[n]
                dve.wait_ge(w_hi, n + 1)
                dve.tensor_tensor(w_lo_sb[:, n % HL, 0:width], raw[:, i % RAW, 0:width],
                                  w_hi_sb[:, n % HL, 0:width].bitcast(F32), ALU.subtract).then_inc(w_lo, 1)

            roots = [0]

            def norm_inv(kind, t, n=1):
                roots[0] += 1
                dve.wait_ge(n_root, roots[0])
                dve.reciprocal(stat(rstd, kind, t, n), stat(rstd, kind, t, n)).then_inc(n_rstd, 1)

            def norm_rows(kind, t, i=0):
                if kind == "x":
                    cols = slice(0, D)
                elif kind == "ffn":
                    cols = slice(i * AW, i * AW + AW)
                else:
                    cols = slice(0, AW) if kind == "attn" else slice(AW, D)
                dst = norm_dst(kind, t, cols)
                if kind == "x":
                    dve.wait_ge(grow_in, 16)
                    dve.wait_ge(n_rstd, t + 1)
                    ins = dve.scalar_tensor_tensor(out=dst, in0=norm_src(kind, t), scalar=stat(rstd, kind, t),
                                                   in1=grow[:, :], op0=ALU.mult, op1=ALU.mult)
                elif kind == "ffn":
                    dve.wait_ge(grow_ffn_in, 16)
                    dve.wait_ge(added, ADD_NO["attno", t, i] + 1)
                    ins = dve.tensor_tensor(dst, xs[:, t, cols], grow_ffn[:, cols], ALU.mult)
                else:
                    dve.wait_ge(grow_out_in, 16)
                    if kind == "attn":
                        dve.wait_ge(o_evac, 2 * t + 2)
                    if kind == "mix":
                        dve.wait_ge(n_ssq, NORM[kind, t] + 1)
                    ins = dve.tensor_tensor(dst, norm_src(kind, t), grow[:, cols], ALU.mult)
                ins.then_inc(n_rows, 1)

            def ht_lo_evac(kind, t, i):
                n = HTN[kind, t, i]
                dve.wait_ge(ht_half, n + 1)
                src, h, l = halves_of(kind, t, i, ht_bank(kind, t, i))
                dve.tensor_tensor(l, src, h.bitcast(F32), ALU.subtract).then_inc(ht_done, 1)

            def x_rows(t):
                norm_inv("x", t)
                norm_rows("x", t)

            def x_lo(t):
                ht_lo_evac("x", t, 0)
                ht_lo_evac("x", t, 1)

            steps = [0]

            def link(ins):
                steps[0] += 1
                ins.then_inc(h_step, 1)
                dve.wait_ge(h_step, steps[0])

            def heads(m):
                t = m % NT
                if m < NT:
                    return (o_sb[:, t, 0:AW].rearrange("p (h d) -> p h d", h=NH),
                            o_sb[:, t, AW:].rearrange("p (h d) -> p h d", h=NH), NH)
                return (zk[:, t, :].rearrange("p (c d) -> p c d", d=HD),
                        sqk[:, t % 2, :].rearrange("p (c d) -> p c d", d=HD), NB * NKV)

            def head_sum(m):
                _, sq, n = heads(m)
                dve.wait_ge(h_ssq, m + 1)
                dve.tensor_reduce(hss[:, m // NT, m % NT, 0:n], sq, AX.X, ALU.add).then_inc(h_sum, 1)

            def rotate(m):
                z, _, n = heads(m)
                w, t = m // NT, m % NT
                dve.wait_ge(h_root, m + 1)
                r = hrs[:, w, t, 0:n]
                link(dve.reciprocal(r, r))
                wait_evac(m)
                link(dve.tensor_tensor(z, z, bc(r.unsqueeze(2), [P, n, HD]), ALU.mult))
                if w == 0:
                    link(dve.tensor_tensor(z, z, bc(gh_sb[:, 0:1, :], [P, n, HD]), ALU.mult))
                else:
                    z4 = z.rearrange("p (b g) d -> p b g d", b=NB)
                    link(dve.tensor_tensor(z4, z4, bc(gh_sb[:, 1:3, :].unsqueeze(2), [P, NB, NKV, HD]), ALU.mult))
                if m:
                    dve.wait_ge(st_lo, m)
                a = t1[:, 0:n * HD].rearrange("p (h d) -> p h d", d=HD)
                b = t2[:, 0:n * HD].rearrange("p (h d) -> p h d", d=HD)
                dve.tensor_tensor(a, z, bc(rope_sb[:, t, 0:1, :], [P, n, HD]), ALU.mult)
                dve.tensor_tensor(b[:, :, 0:HALF], z[:, :, HALF:], bc(rope_sb[:, t, 1:2, 0:HALF], [P, n, HALF]), ALU.mult)
                link(dve.tensor_tensor(b[:, :, HALF:], z[:, :, 0:HALF], bc(rope_sb[:, t, 1:2, HALF:], [P, n, HALF]), ALU.mult))
                dve.tensor_tensor(a, a, b, ALU.add).then_inc(rot, 1)

            def wait_evac(m):
                s = ("out", "A", m) if m < NT else ("out", "B", m - NT)
                dve.wait_ge(out_evac, OUT[s] + 1)

            def stack_lo(m):
                dve.wait_ge(st_hi, m + 1)
                if m < NT:
                    s = stack[:, m % 2]
                    dve.tensor_tensor(s[:, :, 1, :].bitcast(F32R), t1[:, :].rearrange("p (h d) -> p h d", h=NH),
                                      s[:, :, 0, :], ALU.subtract).then_inc(st_lo, 1)
                else:
                    dve.tensor_tensor(kstack(m, 1).bitcast(F32R), k_dup(), kstack(m, 0), ALU.subtract
                                      ).then_inc(st_lo, 1)

            x_rows(0)
            lo(0)
            x_lo(0)
            lo(1)
            lo(2)
            x_rows(1)
            lo(3)
            x_rows(2)
            x_lo(1)
            x_rows(3)
            lo(4)
            x_lo(2)
            dve.wait_ge(tables_in, 16 * 7)
            head_sum(0)
            rotate(0)
            x_lo(3)
            stack_lo(0)
            lo(5)
            head_sum(1)
            rotate(1)
            lo(6)
            stack_lo(1)
            lo(7)
            head_sum(2)
            rotate(2)
            stack_lo(2)
            head_sum(3)
            rotate(3)
            lo(8, 2 * CW)
            stack_lo(3)
            head_sum(4)
            rotate(4)
            lo(9, 2 * CW)
            stack_lo(4)
            head_sum(5)
            rotate(5)
            lo(10, 2 * CW)
            lo(11, 2 * CW)
            stack_lo(5)
            head_sum(6)
            rotate(6)
            lo(12)
            lo(13)
            stack_lo(6)
            head_sum(7)
            rotate(7)
            stack_lo(7)
            lo(14)
            lo(15)

            def blocks(kv):
                dve.wait_ge(out_evac, OUT["cmp_in", kv] + 1)
                for half in range(2):
                    src = par[:, kv, :, :].rearrange("p g (n e) -> p e g n", e=8)[:, :, :, half:half + NC]
                    pe = pe_sb[:, kv, 8 * half:8 * half + 8]
                    last = dve.tensor_tensor(blk[:, kv, 8 * half:8 * half + 8, :, :], src,
                                             bc(pe.unsqueeze(2).unsqueeze(3), [P, 8, NKV, NC]), ALU.add)
                last.then_inc(blk_done, 1)

            blocks(0)
            lo(16)
            lo(17)
            blocks(1)
            for t in range(NT):
                dve.wait_ge(zv_sq, t + 1)
                dve.tensor_reduce(hss[:, 2, t, :], (t1, t2)[t % 2][:, :].rearrange("p (h d) -> p h d", h=NG),
                                  AX.X, ALU.add).then_inc(zv_sum, 1)
                if t == 2:
                    lo(18)
                    lo(19)
            R = NKV * NCP
            dve.wait_ge(kc_root, 1)
            dve.reciprocal(ksum[0:R, 1:2], ksum[0:R, 1:2]).then_inc(kc_rstd, 1)
            dve.wait_ge(kc_rstd, 1)
            j = FILL["kcmp", 0]
            dve.tensor_scalar(kn[:, :, :], bc(ps[0:R, fill_bank(j), 0:HD].unsqueeze(1), [R, 2, HD]),
                              ksum[0:R, 1:2], None, ALU.mult).then_inc(free[j % 4], 1)
            j = FILL["vcmp", 0]
            wait_fill(dve, j)
            dve.wait_ge(pads_made, PADS)
            for g in range(NKV):
                for r in range(GQA):
                    last = dve.tensor_copy(vblk[NCP * r:NCP * r + NCP, g, r * HD:r * HD + HD],
                                           ps[NCP * r:NCP * r + NCP, fill_bank(j), g * HD:g * HD + HD])
            last.then_inc(free[j % 4], 1)
            dve.wait_ge(h_root, 2 * NT + 1)
            link(dve.reciprocal(hrs[:, 2, :, :], hrs[:, 2, :, :]))
            for t in range(NT):
                z = o_sb[:, t, 0:AW].rearrange("p (h d) -> p h d", h=NG)
                dve.tensor_tensor(z, z, bc(hrs[:, 2, t, :].unsqueeze(2), [P, NG, HD]), ALU.mult).then_inc(h_step, 1)
                steps[0] += 1
            for t in range(NT):
                dve.wait_ge(h_step, steps[0] - NT + 1 + t)
                dve.tensor_tensor(o_sb[:, t, 0:AW], o_sb[:, t, 0:AW], gsgu_sb[:, :], ALU.mult).then_inc(zv_norm, 1)
            lo(20)
            dve.wait_ge(masks_made, MASKS)
            for i in range(2):
                j = FILL["cs", i, 0]
                wait_fill(dve, j)
                src = ps[:, fill_bank(j), :].rearrange("p (t r n) -> p t r n", t=2, n=NCP)
                dst = pc[:, 2 * i:2 * i + 2, :, :, :].rearrange("p t g h n -> p t (g h) n")
                dve.tensor_tensor(dst, src, bc(cmp_mask[:, 2 * i:2 * i + 2, :].unsqueeze(2), [P, 2, NH, NCP]),
                                  ALU.add).then_inc(free[j % 4], 1)
            for i in range(2):
                wait_free(dve, FILL["cs", i, 0])
            rows = pc[:, :, :, :, :].rearrange("p t g h n -> p (t g h) n")
            dve.tensor_reduce(cmx[:, :], rows, AX.X, ALU.max).then_inc(cs_step, 1)
            dve.wait_ge(cs_step, 1)
            dve.tensor_scalar(cmx[:, :], cmx[:, :], MAX_FLOOR, None, ALU.max).then_inc(cs_step, 1)
            dve.wait_ge(cs_step, 2)
            dve.tensor_tensor(rows, rows, bc(cmx[:, :].unsqueeze(2), [P, NT * NH, NCP]), ALU.subtract
                              ).then_inc(cs_step, 1)
            dve.wait_ge(g_exp, 1)
            dve.tensor_scalar(glog[:, :, :], glog[:, :, :], 1.0, None, ALU.add).then_inc(g_step, 1)
            dve.wait_ge(g_step, 1)
            dve.reciprocal(glog[:, :, :], glog[:, :, :]).then_inc(g_step, 1)
            for i in range(4):
                j = FILL["sp", i, 0]
                wait_fill(dve, j)
                for g in (2 * i, 2 * i + 1):
                    src = ps[:, fill_bank(j), (g % 2) * 256:(g % 2) * 256 + 256].rearrange("p (c d) -> p c d", c=NT)
                    last = dve.tensor_scalar(o_sb[:, :, g * HD:g * HD + HD], src, spb_sb[:, g:g + 1], None, ALU.add)
                last.then_inc(free[j % 4], 1)

            def mix(t):
                if t == 0:
                    for i in range(4):
                        wait_free(dve, FILL["sp", i, 0])
                dve.wait_ge(out_evac, OUT["out", "D", t] + 1)
                dve.tensor_tensor(o_sb[:, t, AW:], o_sb[:, t, AW:], o_sb[:, t, 0:AW], ALU.mult).then_inc(mixed, 1)

            dve.wait_ge(c_exp, 1)
            dve.wait_ge(g_step, 2)
            gates = glog[:, :, :].rearrange("p t (h n) -> p t h n", n=3)
            dve.tensor_reduce(ccf[:, :], rows, AX.X, ALU.add).then_inc(c_step, 1)
            dve.wait_ge(c_step, 1)
            dve.tensor_scalar(ccf[:, :], ccf[:, :], 1e-20, None, ALU.max).then_inc(c_step, 1)
            dve.wait_ge(c_step, 2)
            dve.reciprocal(ccf[:, :], ccf[:, :]).then_inc(c_step, 1)
            dve.wait_ge(c_step, 3)
            c3 = ccf[:, :].rearrange("p (t h) -> p t h", t=NT)
            dve.tensor_tensor(c3, c3, gates[:, :, :, 0], ALU.mult).then_inc(c_step, 1)
            dve.wait_ge(c_step, 4)
            dve.tensor_tensor(rows, rows, bc(ccf[:, :].unsqueeze(2), [P, NT * NH, NCP]), ALU.mult
                              ).then_inc(c_probs, 1)
            def row_max(v):
                n = P * (STEPS[v][0] + 1)
                if v < PAIRED:
                    if v % 2 == 0:
                        dve.wait_ge(s_done, s_no(v) + 1)
                        dve.tensor_reduce(nmax[:, v:v + 2], ps[:, s_no(v) % SBANKS, 0:2 * P].rearrange(
                            "p (b n) -> p b n", b=NB), AX.X, ALU.max, negate=True).then_inc(s_max, 1)
                else:
                    dve.wait_ge(s_done, s_no(v) + 1)
                    dve.tensor_reduce(nmax[:, v:v + 1], ps[:, s_no(v) % SBANKS, 0:n], AX.X, ALU.max, negate=True
                                      ).then_inc(s_max, 1)

            mix(0)
            mix(1)
            norm_rows("mix", 0)
            norm_rows("mix", 1)
            mix(2)
            ht_lo_evac("mix", 0, 0)
            ht_lo_evac("mix", 1, 0)
            mix(3)
            row_max(0)
            row_max(1)
            norm_rows("mix", 2)
            norm_rows("mix", 3)
            for i in range(2):
                j = FILL["cmpO", i, 0]
                wait_fill(dve, j)
                dve.wait_ge(mixed, i + 1)
                dve.tensor_copy(o_sb[:, i, 0:AW], ps[:, fill_bank(j), :]).then_inc(co_done[0], 1)

            norm_inv("mix", 0, NT)
            lo(21)

            def pt(v):
                n = P * (STEPS[v][0] + 1)
                dve.wait_ge(pt_done, v + 1)
                if v >= 3:
                    dve.wait_ge(pv_done, v - 2)
                dve.tensor_copy(pt_sb[:, v % 3, 0:n], ps[:, 4 + v % 2, 0:n]).then_inc(pt_evac[0], 1)

            osteps = [0]

            def olink(ins):
                osteps[0] += 1
                ins.then_inc(o_step, 1)
                dve.wait_ge(o_step, osteps[0])

            def coefs(t, q):
                hs = slice(4 * q, 4 * q + 4)
                c = coef[:, t, hs, :]
                dve.wait_ge(p_done, 16 * t + 8 * q + 8)
                olink(dve.tensor_scalar(c, psum_p[:, t, hs, :], 1e-20, None, ALU.max))
                olink(dve.reciprocal(c, c))
                olink(dve.tensor_tensor(c, c, gates[:, t, hs, 1:3], ALU.mult))

            def combine(t, q):
                cols = slice(256 * q, 256 * q + 256)
                dve.wait_ge(co_done[t // 2], t % 2 + 1)
                dve.wait_ge(pv_done, 16 * t + 8 * q + 8)
                olink(dve.tensor_tensor(tmp[:, :, cols].rearrange("p b (h d) -> p b h d", h=4),
                                        ps[:, 6 + q, :].rearrange("p (b h d) -> p b h d", b=NB, h=4),
                                        bc(coef[:, t, 4 * q:4 * q + 4, :].rearrange("p h b -> p b h").unsqueeze(3),
                                           [P, NB, 4, HD]), ALU.mult))
                olink(dve.tensor_tensor(tmp[:, 0, cols], tmp[:, 0, cols], tmp[:, 1, cols], ALU.add))
                dve.tensor_tensor(o_sb[:, t, cols], o_sb[:, t, cols], tmp[:, 0, cols], ALU.add).then_inc(o_evac, 1)

            def add(kind, t, h):
                c = slice(h * AW, h * AW + AW)
                dve.wait_ge(job_done, JOB[kind, t, h] + 1)
                if kind == "mixo":
                    dve.wait_ge(x_again[t], 16)
                    dve.wait_ge(n_rstd, NT + 1)
                else:
                    dve.wait_ge(n_rstd, NT + 2 + (0, 0, 1, 2)[t])
                dve.scalar_tensor_tensor(out=xs[:, t, c], in0=ps[:, JOB_BANK[kind, t, h], :],
                                         scalar=stat(rstd, {"mixo": "mix", "attno": "attn"}[kind], t),
                                         in1=xs[:, t, c], op0=ALU.mult, op1=ALU.add).then_inc(added, 1)

            def f_lo(slot, count):
                dve.wait_ge(w_hi, count)
                dve.tensor_tensor(w_lo_sb[:, FS[slot], :], raw[:, slot, :], w_hi_sb[:, FS[slot], :].bitcast(F32),
                                  ALU.subtract).then_inc(w_lo, 1)

            for w in range(NV + LEAD + LAG):
                s = w - LEAD
                k = ENDS.get(s)
                if k in HTN:
                    ht_lo_evac(*k)
                if LEAD <= w < NV:
                    row_max(w)
                if 0 <= s < NV and s % 2 == 0:
                    pt(s)
                if k in ADD_NO:
                    add(*k)
                if w == 2:
                    ht_lo_evac("mix", 2, 0)
                if s == 3:
                    lo(22)
                if s == 11:
                    lo(23)
                if s in (20, 23, 27, 29):
                    lo(24 + (20, 23, 27, 29).index(s))
                if s in (43, 48):
                    f_lo((s - 43) // 5, NS + (s - 43) // 5 + 1)
                if s == 36:
                    norm_inv("attn", 0, 2)
                if s == 52:
                    norm_inv("attn", 2)
                if s % 8 == 6 and 0 <= s < NV:
                    coefs(s // 16, s // 8 % 2)
                if s >= 8 and s % 8 == 1:
                    combine((s - LAG) // 16, (s - LAG) // 8 % 2)
                if s >= 16 and s % 16 == 2 or s == NV + LAG - 1:
                    norm_rows("attn", (s - LAG) // 16 - (s < NV))
                if s in (41, 45, 52, 56):
                    norm_rows("ffn", (s - 41) // 11, {41: 0, 45: 1, 52: 0, 56: 1}[s])

            norm_rows("ffn", 2, 0)
            add("attno", 2, 1)
            ht_lo_evac("attn", 3, 0)
            ht_lo_evac("ffn", 2, 0)
            norm_rows("ffn", 2, 1)
            ht_lo_evac("ffn", 1, 0)
            ht_lo_evac("ffn", 1, 1)
            norm_inv("attn", 3)

            add("attno", 3, 0)
            norm_rows("ffn", 3, 0)
            ht_lo_evac("ffn", 3, 0)
            ht_lo_evac("ffn", 2, 1)
            add("attno", 3, 1)
            norm_rows("ffn", 3, 1)
            ht_lo_evac("ffn", 3, 1)
            f_lo(2, NS + 3)
            f_lo(3, NS + 4)
            dve.wait_ge(n_ssq, len(NORMS))
            r2 = stat(rstd, "ffn", 0, NT)
            dve.tensor_scalar(r2, stat(ssq, "ffn", 0, NT), 1.0 / D, EPS, ALU.mult, ALU.add).then_inc(r2_step, 1)
            dve.wait_ge(r2_step, 1)
            dve.reciprocal(r2, r2).then_inc(r2_step, 1)

            def square(i, j):
                f = i * FR + j
                dve.wait_ge(bank_free, i * FR + (j + 1))
                dve.tensor_tensor(act_sb[:, f, :], act_sb[:, f, :], act_sb[:, f, :], ALU.mult).then_inc(squared, 1)

            def a_low(slot, f, count):
                dve.wait_ge(ah_done, count)
                dve.tensor_tensor(a_lo[:, slot, :], act_sb[:, f, :], a_hi[:, slot, :].bitcast(F32),
                                  ALU.subtract).then_inc(al_done, 1)

            with dve.Fori(0, NF // FR - 1) as i:
                for j in range(FR):
                    square(i, j)
                    f_lo(j, i * FR + (NS + FR + j + 1))
            for j in range(FR):
                square(NF // FR - 1, j)
                f_lo(j, NS + NF + j + 1)
                if j < 2:
                    a_low(j, j, j + 1)
            with dve.Fori(0, NF // FR - 1) as i:
                for j in range(FR):
                    a_low(j % 2, i * FR + (j + 2), i * FR + (j + 3))
                    f_lo(j, i * FR + (NS + NF + FR + j + 1))
            for f in (NF - 2, NF - 1):
                a_low(f % 2, f, f + 1)
            dve.wait_ge(r2_step, 2)

            def result(t, b, n):
                c = slice(b * 512, (b + n) * 512)
                x2 = xs[:, t, c].rearrange("p (b n) -> p b n", b=n)
                dve.scalar_tensor_tensor(out=x2, in0=ps[:, 2 * t + b:2 * t + b + n, :], scalar=stat(rstd, "ffn", t),
                                         in1=x2, op0=ALU.mult, op1=ALU.add).then_inc(final, 1)

            for t in range(NT - 1):
                dve.wait_ge(m_done, t + 1)
                result(t, 0, 2)
            for b in range(2):
                dve.wait_ge(m_done, NT + b)
                result(NT - 1, b, 1)

        @block.tensor
        def _(pe):
            pe.wait_ge(ident_made, 2)

            def rows_t(kind, t, halves=(0, 1)):
                for i in halves:
                    if kind in ("mix", "attn") and i:
                        continue
                    bank = ht_bank(kind, t, i)
                    src = norm_dst(kind, t, slice(i * AW, i * AW + AW))
                    pe.wait_ge(n_rows, ROWN[kind, t, 0 if kind == "x" else i] + 1)
                    filling = (kind, t, i) not in JOB
                    if filling:
                        wait_bank(pe, FILL["x" if kind == "x" else "mixT", t, i])
                    for k in range(4):
                        last = pe.transpose(ps[:, bank, k * P:k * P + P], src[:, k * P:k * P + P], ident[:, :])
                    last.then_inc(filled if filling else job_done, 1)

            def output(g, t):
                s = ("out", g, t)
                o = OUT[s]
                if o >= 4:
                    pe.wait_ge(out_evac, o - 3)
                if g == "A":
                    pe.wait_ge(ht_done, 2 * t + 2)
                for u in range(4):
                    n = SPLIT_NO[g, u]
                    if g == "A" and u == (3, 2, 1, None)[t]:
                        rows_t("x", t + 1)
                    if g == "D" and u == 3 and t == NT - 1:
                        rows_t("mix", 0)
                        rows_t("mix", 1)
                    if t == 0:
                        pe.wait_ge(w_lo, n + 1)
                    wh, wl = slot_w(n, w_hi_sb), slot_w(n, w_lo_sb)
                    for k in range(2):
                        c = (slice(None), 2 * u + k, slice(t * P, t * P + P))
                        last = three(pe, ps[:, o % 4, :], ht_hi[c], ht_lo[c], wh[:, k, :], wl[:, k, :],
                                     u + k == 0, u == 3 and k == 1)
                    if t == NT - 1:
                        last.then_inc(w_used, 1)
                if t < NT - 1:
                    last.then_inc(out_done, 1)

            def gate():
                o = OUT["gate",]
                pe.wait_ge(out_evac, o - 3)
                for kt in range(NK):
                    n = SPLIT_NO["C", kt // 2]
                    pe.wait_ge(w_lo, n + 1)
                    last = three(pe, ps[0:3 * NH, o % 4, :], slot_w(n, w_hi_sb, CW)[:, kt % 2, 0:3 * NH],
                                 slot_w(n, w_lo_sb, CW)[:, kt % 2, 0:3 * NH], ht_hi[:, kt, :], ht_lo[:, kt, :],
                                 kt == 0, kt == NK - 1)
                last.then_inc(out_done, 1)

            def gate_back():
                j = FILL["gateT", 0]
                wait_bank(pe, j)
                pe.wait_ge(out_evac, OUT["gate",] + 1)
                for t in range(NT):
                    last = pe.transpose(ps[:, fill_bank(j), t * 3 * NH:(t + 1) * 3 * NH], gate_t[:, t * P:t * P + P],
                                        ident[0:3 * NH, 0:3 * NH])
                last.then_inc(filled, 1)

            def cmp_in(kv):
                o = OUT["cmp_in", kv]
                pe.wait_ge(out_evac, o - 3)
                for kt in range(NK):
                    n = SPLIT_NO["C", kt // 2]
                    c = slice(3 * NH + kv * P, 3 * NH + kv * P + P)
                    last = three(pe, ps[:, o % 4, :], slot_w(n, w_hi_sb, CW)[:, kt % 2, c],
                                 slot_w(n, w_lo_sb, CW)[:, kt % 2, c], ht_hi[:, kt, :], ht_lo[:, kt, :],
                                 kt == 0, kt == NK - 1)
                    if kv == 1 and kt % 2 == 1:
                        last.then_inc(w_used, 1)
                if kv == 0:
                    last.then_inc(out_done, 1)

            def stack_t(m):
                kind, t = ("q", m) if m < NT else ("k", m - NT)
                pe.wait_ge(st_lo, m + 1)
                s = stack[:, m % 2].rearrange("p h e d -> p (h e d)")
                for i in range(FILLS[kind]):
                    j = FILL[kind, t, i]
                    wait_bank(pe, j)
                    for k in range(4):
                        src = s[:, (4 * i + k) * P:(4 * i + k + 1) * P] if i < 2 else o_sb[:, t, k * P:k * P + P]
                        last = pe.transpose(ps[:, fill_bank(j), k * P:k * P + P], src, ident[:, :])
                    last.then_inc(filled, 1)

            def spatial(i):
                j = FILL["sp", i, 0]
                wait_bank(pe, j)
                if i == 0:
                    pe.wait_ge(spw_made, 1)
                    pe.wait_ge(zv_norm, NT)
                for g in (2 * i, 2 * i + 1):
                    mm = pe.matmul(ps[:, fill_bank(j), (g % 2) * 256:(g % 2) * 256 + 256], spw_sb[:, g, :],
                                   o_sb[:, :, g * HD:g * HD + HD], start=True, stop=True)
                mm.then_inc(filled, 1)

            def hidden(kv):
                f = FILL["hid", kv, 0]
                pe.wait_ge(blk_done, kv + 1)
                wait_bank(pe, f)
                for u in range(4):
                    i = STREAM.index(("direct", kv, u))
                    pe.wait_ge(raw_in[i % RAW], 16 * (i // RAW + 1))
                    for j in range(4):
                        last = pe.matmul(ps[0:NKV * NC, fill_bank(f), 0:CMP_HID],
                                         blk[:, kv, 4 * u + j, :, :].rearrange("p g n -> p (g n)"),
                                         raw[:, i % RAW, j * CMP_HID:(j + 1) * CMP_HID],
                                         start=u + j == 0, stop=u == 3 and j == 3)
                    last.then_inc(filled if u == 3 else cw_used, 1)

            def hidden_t(kv):
                f = FILL["hidT", kv, 0]
                wait_bank(pe, f)
                wait_free(pe, FILL["hid", kv, 0])
                for half in range(2):
                    last = pe.transpose(ps[:, fill_bank(f), half * P:half * P + NKV * NC],
                                        hid[:, kv, half * P:half * P + P], ident[0:NKV * NC, 0:NKV * NC])
                last.then_inc(filled, 1)

            def kcmp():
                j = FILL["kcmp", 0]
                wait_bank(pe, j)
                wait_free(pe, FILL["hidT", 0, 0])
                for half in range(2):
                    mm = pe.matmul(ps[0:NKV * NCP, fill_bank(j), 0:HD], hid_k[:, half, :, :].rearrange("p g n -> p (g n)"),
                                   cw2_sb[:, 0, half, :], start=half == 0, stop=half == 1)
                mm.then_inc(filled, 1)

            def vcmp():
                j = FILL["vcmp", 0]
                wait_bank(pe, j)
                wait_free(pe, FILL["hidT", 1, 0])
                for g in range(NKV):
                    for half in range(2):
                        mm = pe.matmul(ps[:, fill_bank(j), g * HD:g * HD + HD],
                                       hid_v[:, half, g, :, :].rearrange("p r n -> p (r n)"),
                                       cw2_sb[:, 1, half, :], start=half == 0, stop=half == 1)
                mm.then_inc(filled, 1)

            def kcmp_t():
                j = FILL["kcmpT", 0]
                wait_bank(pe, j)
                wait_free(pe, FILL["kcmp", 0])
                R = NKV * NCP
                pe.transpose(ps[:, fill_bank(j), 0:R], kn[:, :, :].rearrange("p e d -> p (e d)"), ident[0:R, 0:R]
                             ).then_inc(filled, 1)

            def cmp_scores(i):
                j = FILL["cs", i, 0]
                wait_bank(pe, j)
                wait_free(pe, FILL["kcmpT", 0])
                for t in (2 * i, 2 * i + 1):
                    for pair in range(NH // 2):
                        c = ((t % 2) * (NH // 2) + pair) * 2 * NCP
                        mm = pe.matmul(ps[:, fill_bank(j), c:c + 2 * NCP], qcT[:, pair, t * P:t * P + P],
                                       kcT[:, 2 * pair // GQA, :, :].rearrange("p e n -> p (e n)"),
                                       start=True, stop=True)
                mm.then_inc(filled, 1)

            def cmp_probs_t(i):
                j = FILL["cmpPT", i, 0]
                wait_bank(pe, j)
                pe.wait_ge(c_probs, 1)
                for k in range(4):
                    t, g = 2 * i + k // 2, k % 2
                    mm = pe.transpose(ps[:, fill_bank(j), k * P:k * P + P],
                                      pc[:, t, g, :, :].rearrange("p h n -> p (h n)"), ident[:, :])
                mm.then_inc(filled, 1)

            def cmp_values(t):
                j = FILL["cmpO", t, 0]
                wait_bank(pe, j)
                wait_free(pe, FILL["cmpPT", t // 2, 0])
                for g in range(NKV):
                    mm = pe.matmul(ps[:, fill_bank(j), g * 256:g * 256 + 256], pcT[:, 2 * t + g, :],
                                   vblk[:, g, :], start=True, stop=True)
                mm.then_inc(filled, 1)

            def scores(v):
                t, h, b = STEPS[v]
                n = P * (t + 1)
                if v < PAIRED and v % 2:
                    return
                if s_before(v) is not None:
                    pe.wait_ge(p_done, s_before(v) + 1)
                bank, q, g = s_no(v) % SBANKS, qT[:, h, t * P:t * P + P], h // GQA
                if v < PAIRED:
                    out = ps[:, bank, 0:NB * P].rearrange("p (b n) -> p b n", b=NB)
                    k, diagonal, mask = kT[:, :, g, :, 0:P], out, causal16[:, :, :]
                    k = [k[:, :, 0, :], k[:, :, 1, :]]
                else:
                    out, diagonal, mask = ps[:, bank, 0:n], ps[:, bank, n - P:n], causal16[:, 0, :]
                    k = [kT[:, b, g, 0, 0:n], kT[:, b, g, 1, 0:n]]
                pe.matmul(out, q, k[0], start=True, stop=False)
                pe.matmul(out, q, k[1], start=False, stop=False)
                pe.matmul(diagonal, ident16[:, :], mask, start=False, stop=True).then_inc(s_done, 1)

            def first_scores():
                pe.wait_ge(masks_made, MASKS)
                pe.wait_ge(out_evac, max(o for o in range(len(OUTS)) if o % 4 == 0) + 1)
                for v in range(LEAD):
                    scores(v)

            RUN = {"x": lambda t: rows_t("x", t), "out": output, "q": stack_t, "k": lambda t: stack_t(NT + t),
                   "gate": gate, "gateT": gate_back, "cmp_in": cmp_in, "sp": spatial, "hid": hidden, "hidT": hidden_t,
                   "kcmp": kcmp, "vcmp": vcmp, "kcmpT": kcmp_t, "mixT": lambda t: rows_t("mix", t),
                   "cs": cmp_scores, "s": first_scores, "cmpPT": cmp_probs_t, "cmpO": cmp_values}
            for _ in range(WARM):
                pe.transpose(ps[:, 3, 0:P], ident[:, :], ident[:, :])
            for s in SEQUENCE:
                if s[:2] not in (("mixT", 0), ("mixT", 1)) and (s[0] != "x" or s[1] == 0):
                    RUN[s[0]](*s[1:])

            def probs_t(v):
                pe.wait_ge(p_done, v + 1)
                if v >= 2:
                    pe.wait_ge(pt_evac[v % 2], v // 2)
                else:
                    wait_free(pe, LAST_FILL[v % 2])
                for k in range(STEPS[v][0] + 1):
                    mm = pe.transpose(ps[:, 4 + v % 2, k * P:k * P + P], p_sb[:, v % 3, k * P:k * P + P], ident[:, :])
                mm.then_inc(pt_done, 1)

            def values(v):
                t, h, b = STEPS[v]
                pe.wait_ge(pt_evac[v % 2], v // 2 + 1)
                if v in (0, 8):
                    wait_free(pe, LAST_FILL[2 + h // 4])
                if h % 4 == 0 and b == 0 and t > 0:
                    pe.wait_ge(o_step, 5 * (2 * (t - 1) + h // 4) + 4)
                g, c = h // GQA, (b * 4 + h % 4) * HD
                for k in range(t + 1):
                    mm = pe.matmul(ps[:, 6 + h // 4, c:c + HD], pt_sb[:, v % 3, k * P:k * P + P],
                                   v_sb[:, k, b, g * HD:g * HD + HD], start=k == 0, stop=k == t)
                mm.then_inc(pv_done, 1)

            LAST_FILL = [max(j for j in range(len(FILL)) if j % 4 == b) for b in range(4)]

            def project(kind, t, half, c):
                n = SPLIT_NO[f"O{half}", (0 if kind == "mixo" else 2) + c // 2]
                if c % 2 == 0:
                    pe.wait_ge(w_lo, n + 1)
                k0 = 4 if kind == "mixo" else 0
                if c == 0 and half == 0:
                    pe.wait_ge(ht_done, HTN["mix" if kind == "mixo" else "attn", t, 0] + 1)
                rows = (slice(None), k0 + c, slice(t * P, t * P + P))
                return three(pe, ps[:, JOB_BANK[kind, t, half], :], ht_hi[rows], ht_lo[rows],
                             slot_w(n, w_hi_sb)[:, c % 2, :], slot_w(n, w_lo_sb)[:, c % 2, :], c == 0, c == 3)

            def job(k, c):
                before = [p for p in JOB_KEY[:JOB[k]] if JOB_BANK[p] == JOB_BANK[k]]
                if c == 0 and before:
                    job_taken(pe, before[-1])
                if k in HTN:
                    rows_t(k[0], k[1], (k[2],))
                else:
                    mm = project(*k, c)
                    if c == 3:
                        mm.then_inc(job_done, 1)

            pe.wait_ge(out_evac, len(OUTS))
            for v in range(NV + LAG):
                if v + LEAD < NV:
                    scores(v + LEAD)
                if v in CHUNKS and CHUNKS[v][0] in HTN:
                    job(*CHUNKS[v])
                if v < NV:
                    probs_t(v)
                product = CHUNKS[v] if v in CHUNKS and CHUNKS[v][0] in ADD_NO else None
                if product and product[1] > 0:
                    job(*product)
                if v >= LAG:
                    values(v - LAG)
                if product and product[1] == 0:
                    job(*product)
            pe.wait_ge(p_done, NV)
            for b in range(NB):
                pe.wait_ge(pt_evac[b], NV // 2)
            for k in TAIL[:-1]:
                for c in range(4 if k in ADD_NO else 1):
                    job(k, c)

            pe.wait_ge(o_evac, 2 * NT)

            def hidden_part(j, ks, rows=slice(0, SEQ)):
                for k in ks:
                    c = slice(k * P, k * P + P)
                    mm = three(pe, ps[:, 4 + j, rows], w_hi_sb[:, FS[j], c], w_lo_sb[:, FS[j], c],
                               ht_hi[:, k, rows], ht_lo[:, k, rows], k == 0, k == NK - 1)
                return mm

            early, late = slice(0, 2 * P), slice(2 * P, SEQ)
            pe.wait_ge(w_lo, NS + 1)
            pe.wait_ge(ht_done, HTN["ffn", 1, 1] + 1)
            hidden_part(0, range(NK), early)
            job(("ffn", NT - 1, 1), 0)
            pe.wait_ge(ht_done, HTN["ffn", NT - 1, 0] + 1)
            hidden_part(0, range(4), late)
            pe.wait_ge(w_lo, NS + 2)
            hidden_part(1, range(4))
            pe.wait_ge(ht_done, len(HT))
            hidden_part(0, range(4, NK), late).then_inc(w_used, 1)
            hidden_part(1, range(4, NK)).then_inc(w_used, 1)
            for j in range(2, FR):
                pe.wait_ge(w_lo, NS + j + 1)
                hidden_part(j, range(NK)).then_inc(w_used, 1)
            with pe.Fori(1, NF // FR) as i:
                for j in range(FR):
                    pe.wait_ge(w_lo, i * FR + (NS + j + 1))
                    hidden_part(j, range(NK)).then_inc(w_used, 1)

            def second(j, w_count, a_count, first=False, final_unit=False):
                pe.wait_ge(w_lo, w_count)
                pe.wait_ge(al_done, a_count)
                for t in range(NT):
                    if first and t == NT // 2:
                        pe.wait_ge(bank_free, NF)
                    rows = slice(t * P, t * P + P)
                    for b in range(2):
                        n = slice(b * 512, b * 512 + 512)
                        mm = three(pe, ps[:, 2 * t + b, :], a_hi[:, j % 2, rows], a_lo[:, j % 2, rows],
                                   w_hi_sb[:, FS[j], n], w_lo_sb[:, FS[j], n], first, final_unit)
                        if final_unit and (b == 1 or t == NT - 1):
                            mm.then_inc(m_done, 1)
                if not final_unit:
                    mm.then_inc(w_used, 1)

            for j in range(FR):
                second(j, NS + NF + j + 1, j + 1, first=j == 0)
            with pe.Fori(1, NF // FR - 1) as i:
                for j in range(FR):
                    second(j, i * FR + (NS + NF + j + 1), i * FR + (j + 1))
            for j in range(FR):
                f = NF - FR + j
                second(j, NS + NF + f + 1, f + 1, final_unit=j == FR - 1)


def rope_tables():
    import numpy as np

    inv = np.float32(10000.0) ** (-np.arange(HALF, dtype=np.float32) / np.float32(HALF))
    ang = np.arange(SEQ, dtype=np.float32)[:, None] * inv[None, :]
    c, s = np.cos(ang), np.sin(ang)
    table = np.stack([np.concatenate([c, c], 1), np.concatenate([-s, s], 1)], 1).astype(np.float32)
    return table.reshape(NT, P, 2, HD).transpose(1, 0, 2, 3)


def layouts(i):
    import numpy as np

    w = i["w_in"][0]
    q_end = AW
    kv = {n: slice(q_end + k * P, q_end + (k + 1) * P) for k, n in
          enumerate(["kc", "vc", "k_sel", "v_sel", "k_win", "v_win"])}
    g0 = q_end + 6 * P
    zu, zv = slice(g0 + 3 * NH, g0 + 3 * NH + AW), slice(g0 + 3 * NH + AW, g0 + 3 * NH + 2 * AW)

    def units(a, order=range(NK)):
        return a.reshape(NK, P, -1)[list(order)].reshape(4, 2, P, -1).transpose(0, 2, 1, 3).reshape(4, P, -1)

    group = {"A": w[:, 0:AW], "B": w[:, slice(kv["k_sel"].start, kv["v_win"].stop)],
             "C": np.concatenate([w[:, g0:g0 + 3 * NH], w[:, kv["kc"]], w[:, kv["vc"]]], 1),
             "E": w[:, zv], "D": w[:, zu]}
    wo = i["w_out"][0]
    return {
        "x": i["x"][0].reshape(NT, P, D),
        "w512": np.concatenate([units(group[g]) for g in "ABED"]
                               + [units(wo[:, h * 512:h * 512 + 512], K_ORDER) for h in range(2)]),
        "w_c": units(group["C"]),
        "cmp_w1": i["cmp_w1"][0].reshape(2, 4, 4, P, CMP_HID).transpose(0, 1, 3, 2, 4).reshape(2, 4, P, UW),
        "cmp_w2": i["cmp_w2"][0].reshape(2, 2, P, HD).transpose(2, 0, 1, 3),
        "cmp_pe": i["cmp_pe"][0].reshape(2, 16, P).transpose(2, 0, 1),
        "sp_w": i["sp_w"][0].transpose(2, 0, 1),
        "sp_b": i["sp_b"][0].T,
        "g_rows": np.concatenate([i["g_mix_norm"], i["g_out"], i["g_ffn_norm"]], 0),
        "g_heads": np.concatenate([i["g_q"], i["g_k"][0, 1:3]], 0),
        "g_sgu": i["g_sgu"].reshape(1, NG * HD),
        "g_kc": np.concatenate([i["g_k"][0, 0], i["g_k"][0, 0]])[:, None],
        "rope": rope_tables(),
        "w_ff1": i["w_ff1"][0].reshape(NK, P, NF, P).transpose(2, 1, 0, 3).reshape(NF, P, D),
        "w_ff2": i["w_ff2"][0].reshape(NF, P, D),
    }


def kernel(**inputs):
    import numpy as np
    import concourse.bacc as bacc
    from concourse.bass_utils import run_bass_kernel_spmd

    nc = bacc.Bacc("TRN2", target_bir_lowering=False, num_devices=1)
    sent, args = {}, {}
    for name, a in layouts({k: np.asarray(v) for k, v in inputs.items()}).items():
        sent[f"in_{name}"] = np.ascontiguousarray(a)
        args[name] = nc.dram_tensor(f"in_{name}", a.shape, F32, kind="ExternalInput").ap()
    y = nc.dram_tensor("out_y", (NT, P, D), F32, kind="ExternalOutput").ap()
    hybrid_block(nc, **args, y=y)
    r = run_bass_kernel_spmd(nc, [sent], core_ids=[0])
    return r.results[0]["out_y"].reshape(1, SEQ, D)
```
